# Optimizing a Trainium2 kernel written in Bass

```python
import math
import jax, jax.numpy as jnp
from jax import lax
import numpy as np

D_MODEL = 1024
BATCH = 1
SEQ = 256
DEPTH = 2

HEAD_DIM = 64
N_HEADS = 4
MIX_WIDTH = N_HEADS * HEAD_DIM
N_MIXERS = 4
ROPE_THETA = 500000.0
ROPE_FRACTION_DEN = 4
Q_BLOCK = 128
SPARSE_Q_BLOCK = 32
DIFF_DIM = HEAD_DIM // 2
MOBA_BLOCK = 256
MOBA_TOPK = 3
NSA_CMP_LEN = 32
NSA_CMP_STRIDE = 16
NSA_SLC_BLOCK = 64
NSA_TOPN = 16
NSA_WINDOW = 512
NSA_KV_DIM = HEAD_DIM
FFN_HIDDEN = -(-8 * D_MODEL // (3 * 256)) * 256
NEG_INF = -1e30
BIG = 1e30
RMS_EPS = 1e-6
IN_SPLITS = (MIX_WIDTH,) * 10 + (NSA_KV_DIM,) * 6 + (3 * N_HEADS,)
IN_COLS = sum(IN_SPLITS)

kernel_name = "hybrid_gated_sparse_attention_trunk"

def _rms_norm(x, g):
    xf = x.astype(jnp.float32)
    y = xf * lax.rsqrt(jnp.mean(xf * xf, axis=-1, keepdims=True) + RMS_EPS)
    return (y * g.astype(jnp.float32)).astype(x.dtype)

def _rope(x, pos):
    d = x.shape[-1]
    r = d // ROPE_FRACTION_DEN
    half = r // 2
    inv = ROPE_THETA ** (-jnp.arange(half, dtype=jnp.float32) * 2.0 / r)
    ang = pos.astype(jnp.float32)[:, None] * inv[None, :]
    cos, sin = jnp.cos(ang), jnp.sin(ang)
    xf = x.astype(jnp.float32)
    x1, x2 = xf[..., :half], xf[..., half:r]
    out = jnp.concatenate([x1 * cos - x2 * sin, x2 * cos + x1 * sin, xf[..., r:]], axis=-1)
    return out.astype(x.dtype)

def _heads(t):
    b, s, _ = t.shape
    return t.reshape(b, s, N_HEADS, -1).transpose(0, 2, 1, 3)

def _merge_heads(o):
    b, h, s, d = o.shape
    return o.transpose(0, 2, 1, 3).reshape(b, s, h * d)

def _masked_softmax(s, mask):
    s = jnp.where(mask, s.astype(jnp.float32), NEG_INF)
    m = jnp.max(s, axis=-1, keepdims=True)
    e = jnp.where(mask, jnp.exp(s - m), 0.0)
    return e / jnp.maximum(jnp.sum(e, axis=-1, keepdims=True), 1e-30)

def _sweep(fn, seq, blk):
    return lax.map(fn, jnp.arange(seq // blk, dtype=jnp.int32) * blk)

def _unblock(y):
    n, b, h, c, d = y.shape
    return jnp.transpose(y, (1, 2, 0, 3, 4)).reshape(b, h, n * c, d)

def _stick_breaking(q, k, v):
    b, h, s, d = q.shape
    scale = 1.0 / math.sqrt(d)
    kpos = jnp.arange(s, dtype=jnp.int32)

    def blk(c0):
        qb = lax.dynamic_slice_in_dim(q, c0, Q_BLOCK, axis=2)
        z = jnp.einsum('bhqd,bhkd->bhqk', qb, k).astype(jnp.float32) * scale
        qpos = c0 + jnp.arange(Q_BLOCK, dtype=jnp.int32)
        mask = kpos[None, :] < qpos[:, None]
        log1m = jnp.where(mask, jax.nn.log_sigmoid(-z), 0.0)
        between = lax.cumsum(log1m, axis=3, reverse=True) - log1m
        a = jnp.where(mask, jnp.exp(jax.nn.log_sigmoid(z) + between), 0.0)
        return jnp.einsum('bhqk,bhkd->bhqd', a.astype(v.dtype), v)

    return _unblock(_sweep(blk, s, Q_BLOCK))

def _diff_attention(q1, q2, k1, k2, v, lam):
    b, h, s, d = q1.shape
    scale = 1.0 / math.sqrt(d)
    kpos = jnp.arange(s, dtype=jnp.int32)

    def blk(c0):
        qpos = c0 + jnp.arange(Q_BLOCK, dtype=jnp.int32)
        mask = kpos[None, :] <= qpos[:, None]
        q1b = lax.dynamic_slice_in_dim(q1, c0, Q_BLOCK, axis=2)
        q2b = lax.dynamic_slice_in_dim(q2, c0, Q_BLOCK, axis=2)
        p1 = _masked_softmax(jnp.einsum('bhqd,bhkd->bhqk', q1b, k1).astype(jnp.float32) * scale, mask)
        p2 = _masked_softmax(jnp.einsum('bhqd,bhkd->bhqk', q2b, k2).astype(jnp.float32) * scale, mask)
        p = p1 - lam * p2
        return jnp.einsum('bhqk,bhkd->bhqd', p.astype(v.dtype), v)

    return _unblock(_sweep(blk, s, Q_BLOCK))

def _moba(q, k, v):
    b, h, s, d = q.shape
    scale = 1.0 / math.sqrt(d)
    nb = -(-s // MOBA_BLOCK)
    pad = nb * MOBA_BLOCK - s
    kb = jnp.pad(k, ((0, 0), (0, 0), (0, pad), (0, 0))).reshape(b, h, nb, MOBA_BLOCK, d)
    vb = jnp.pad(v, ((0, 0), (0, 0), (0, pad), (0, 0))).reshape(b, h, nb, MOBA_BLOCK, d)
    kmean = jnp.mean(kb.astype(jnp.float32), axis=3).astype(k.dtype)
    ksel = min(MOBA_TOPK, nb - 1)
    bi = jnp.arange(b)[:, None, None, None]
    hi = jnp.arange(h)[None, :, None, None]
    blk_ids = jnp.arange(nb, dtype=jnp.int32)
    off = jnp.arange(MOBA_BLOCK, dtype=jnp.int32)
    L = MOBA_BLOCK
    C = SPARSE_Q_BLOCK

    def blk(c0):
        qb = lax.dynamic_slice_in_dim(q, c0, C, axis=2)
        qpos = c0 + jnp.arange(C, dtype=jnp.int32)
        ob = c0 // MOBA_BLOCK
        k_own = lax.dynamic_index_in_dim(kb, ob, axis=2, keepdims=False)
        v_own = lax.dynamic_index_in_dim(vb, ob, axis=2, keepdims=False)
        s_own = jnp.einsum('bhqd,bhkd->bhqk', qb, k_own).astype(jnp.float32) * scale
        m_own = jnp.broadcast_to((ob * MOBA_BLOCK + off)[None, :] <= qpos[:, None], s_own.shape)
        if ksel == 0:
            p_own = _masked_softmax(s_own, m_own).astype(v.dtype)
            return jnp.einsum('bhqk,bhkd->bhqd', p_own, v_own)
        gate = jnp.einsum('bhqd,bhnd->bhqn', qb, kmean).astype(jnp.float32)
        gate = jnp.where(blk_ids < ob, gate, NEG_INF)
        _, idx = lax.top_k(gate, ksel)
        valid = idx < ob
        k_sel = kb[bi, hi, idx]
        v_sel = vb[bi, hi, idx]
        s_sel = jnp.einsum('bhqd,bhqnkd->bhqnk', qb, k_sel).astype(jnp.float32) * scale
        m_sel = jnp.broadcast_to(valid[..., None], s_sel.shape)
        sc = jnp.concatenate([s_sel.reshape(b, h, C, ksel * L), s_own], axis=-1)
        mk = jnp.concatenate([m_sel.reshape(b, h, C, ksel * L), m_own], axis=-1)
        p = _masked_softmax(sc, mk).astype(v.dtype)
        p_sel = p[..., :ksel * L].reshape(b, h, C, ksel, L)
        p_own = p[..., ksel * L:]
        return (jnp.einsum('bhqnk,bhqnkd->bhqd', p_sel, v_sel)
                + jnp.einsum('bhqk,bhkd->bhqd', p_own, v_own))

    return _unblock(_sweep(blk, s, C))

def _nsa(q, kc_tok, vc_tok, ks, vs, kw, vw, gates, kn_g, cmp_pe, cmp_w):
    b, h, s, d = q.shape
    scale = 1.0 / math.sqrt(d)
    pos = jnp.arange(s, dtype=jnp.int32)
    C = SPARSE_Q_BLOCK
    nc = (s - NSA_CMP_LEN) // NSA_CMP_STRIDE + 1
    cstart = NSA_CMP_STRIDE * jnp.arange(nc, dtype=jnp.int32)
    widx = cstart[:, None] + jnp.arange(NSA_CMP_LEN, dtype=jnp.int32)[None, :]
    cmp_end = cstart + (NSA_CMP_LEN - 1)

    def compress(t, pe, w):
        blocks = t[:, widx] + pe
        return blocks.reshape(b, nc, NSA_CMP_LEN * d) @ w

    kc = _rope(_rms_norm(compress(kc_tok, cmp_pe[0], cmp_w[0]), kn_g[0]), cmp_end)
    vc = compress(vc_tok, cmp_pe[1], cmp_w[1])
    ns = s // NSA_SLC_BLOCK
    ntop = min(NSA_TOPN, ns)
    ks = _rope(_rms_norm(ks, kn_g[1]), pos)
    ksb = ks.reshape(b, ns, NSA_SLC_BLOCK, d)
    vsb = vs.reshape(b, ns, NSA_SLC_BLOCK, d)
    sstart = NSA_SLC_BLOCK * jnp.arange(ns, dtype=jnp.int32)
    overlap = jnp.clip(jnp.minimum(cstart[:, None] + NSA_CMP_LEN, sstart[None, :] + NSA_SLC_BLOCK)
                       - jnp.maximum(cstart[:, None], sstart[None, :]), 0, None)
    cmp_to_slc = overlap.astype(jnp.float32) / NSA_CMP_STRIDE
    slc_ids = jnp.arange(ns, dtype=jnp.int32)
    slc_off = jnp.arange(NSA_SLC_BLOCK, dtype=jnp.int32)
    bi = jnp.arange(b)[:, None, None]
    kw = _rope(_rms_norm(kw, kn_g[2]), pos)
    kw_pad = jnp.pad(kw, ((0, 0), (NSA_WINDOW, 0), (0, 0)))
    vw_pad = jnp.pad(vw, ((0, 0), (NSA_WINDOW, 0), (0, 0)))
    woff = jnp.arange(NSA_WINDOW + C, dtype=jnp.int32)

    def blk(c0):
        qb = lax.dynamic_slice_in_dim(q, c0, C, axis=2)
        qpos = c0 + jnp.arange(C, dtype=jnp.int32)
        s_c = jnp.einsum('bhqd,bnd->bhqn', qb, kc).astype(jnp.float32) * scale
        p_c = _masked_softmax(s_c, cmp_end[None, :] <= qpos[:, None])
        o_c = jnp.einsum('bhqn,bnd->bhqd', p_c.astype(vc.dtype), vc)
        imp = jnp.einsum('bhqn,nj->bqj', p_c, cmp_to_slc)
        cur = qpos // NSA_SLC_BLOCK
        forced = ((slc_ids[None, :] == 0) | (slc_ids[None, :] == cur[:, None])
                  | (slc_ids[None, :] == cur[:, None] - 1))
        allowed = slc_ids[None, :] <= cur[:, None]
        score = jnp.where(allowed, jnp.where(forced, BIG, imp), NEG_INF)
        _, idx = lax.top_k(score, ntop)
        k_sel = ksb[bi, idx]
        v_sel = vsb[bi, idx]
        kpos_sel = idx[..., None] * NSA_SLC_BLOCK + slc_off
        m_s = (kpos_sel <= qpos[None, :, None, None]).reshape(b, 1, C, ntop * NSA_SLC_BLOCK)
        s_s = jnp.einsum('bhqd,bqnkd->bhqnk', qb, k_sel).astype(jnp.float32) * scale
        p_s = _masked_softmax(s_s.reshape(b, h, C, ntop * NSA_SLC_BLOCK), m_s)
        p_s = p_s.reshape(b, h, C, ntop, NSA_SLC_BLOCK).astype(v_sel.dtype)
        o_s = jnp.einsum('bhqnk,bqnkd->bhqd', p_s, v_sel)
        kwb = lax.dynamic_slice_in_dim(kw_pad, c0, NSA_WINDOW + C, axis=1)
        vwb = lax.dynamic_slice_in_dim(vw_pad, c0, NSA_WINDOW + C, axis=1)
        kp = c0 - NSA_WINDOW + woff
        m_w = ((kp[None, :] <= qpos[:, None]) & (kp[None, :] > qpos[:, None] - NSA_WINDOW)
               & (kp[None, :] >= 0))
        s_w = jnp.einsum('bhqd,bkd->bhqk', qb, kwb).astype(jnp.float32) * scale
        o_w = jnp.einsum('bhqk,bkd->bhqd', _masked_softmax(s_w, m_w).astype(vwb.dtype), vwb)
        return (o_c, o_s, o_w)

    o_c, o_s, o_w = _sweep(blk, s, C)
    return gates[0] * _unblock(o_c) + gates[1] * _unblock(o_s) + gates[2] * _unblock(o_w)

def setup_inputs(seed: int = 0) -> dict:
    key = jax.random.key(seed)
    ks = jax.random.split(key, 21)
    D, L = D_MODEL, DEPTH

    def nrm(k, shape, scale):
        return jax.random.normal(k, shape, jnp.float32) * scale

    def gain(k, shape):
        return 1.0 + nrm(k, shape, 0.05)

    return {
        "x": nrm(ks[0], (BATCH, SEQ, D), 1.0),
        "attn_norm_g": gain(ks[1], (L, D)),
        "w_in": nrm(ks[2], (L, D, IN_COLS), D ** -0.5),
        "diff_qn_g": gain(ks[3], (L, DIFF_DIM)),
        "diff_kn_g": gain(ks[4], (L, DIFF_DIM)),
        "diff_lam": nrm(ks[5], (L, 4, DIFF_DIM), 0.1),
        "diff_subln_g": gain(ks[6], (L, HEAD_DIM)),
        "moba_qn_g": gain(ks[7], (L, HEAD_DIM)),
        "moba_kn_g": gain(ks[8], (L, HEAD_DIM)),
        "nsa_qn_g": gain(ks[9], (L, HEAD_DIM)),
        "nsa_kn_g": gain(ks[10], (L, 3, NSA_KV_DIM)),
        "nsa_cmp_pe": nrm(ks[11], (L, 2, NSA_CMP_LEN, NSA_KV_DIM), 0.1),
        "nsa_cmp_w": nrm(ks[12], (L, 2, NSA_CMP_LEN * NSA_KV_DIM, NSA_KV_DIM), (NSA_CMP_LEN * NSA_KV_DIM) ** -0.5),
        "w_gate": nrm(ks[13], (L, N_MIXERS, D, D), D ** -0.5),
        "b_gate": nrm(ks[14], (L, N_MIXERS, D), 0.01),
        "w_branch": nrm(ks[15], (L, N_MIXERS, MIX_WIDTH, D), MIX_WIDTH ** -0.5),
        "w_out": nrm(ks[16], (L, D, D), D ** -0.5),
        "ffn_norm_g": gain(ks[17], (L, D)),
        "w_ffn_gate": nrm(ks[18], (L, D, FFN_HIDDEN), D ** -0.5),
        "w_ffn_up": nrm(ks[19], (L, D, FFN_HIDDEN), D ** -0.5),
        "w_ffn_down": nrm(ks[20], (L, FFN_HIDDEN, D), FFN_HIDDEN ** -0.5),
    }

def reference(x, attn_norm_g, w_in, diff_qn_g, diff_kn_g, diff_lam, diff_subln_g,
              moba_qn_g, moba_kn_g, nsa_qn_g, nsa_kn_g, nsa_cmp_pe, nsa_cmp_w,
              w_gate, b_gate, w_branch, w_out, ffn_norm_g, w_ffn_gate, w_ffn_up, w_ffn_down):
    b, s, _ = x.shape
    pos = jnp.arange(s, dtype=jnp.int32)
    split_at = [int(o) for o in np.cumsum(IN_SPLITS)[:-1]]
    for l in range(DEPTH):
        xn = _rms_norm(x, attn_norm_g[l])
        (sb_q, sb_k, sb_v, df_q, df_k, df_v, mb_q, mb_k, mb_v, ns_q,
         ns_kc, ns_vc, ns_ks, ns_vs, ns_kw, ns_vw, ns_g) = jnp.split(xn @ w_in[l], split_at, axis=-1)

        o_a = _stick_breaking(_heads(sb_q), _heads(sb_k), _heads(sb_v))

        lam_init = 0.8 - 0.6 * math.exp(-0.3 * l)
        dq = df_q.reshape(b, s, N_HEADS, 2, DIFF_DIM).transpose(3, 0, 2, 1, 4)
        dk = df_k.reshape(b, s, N_HEADS, 2, DIFF_DIM).transpose(3, 0, 2, 1, 4)
        dq = _rope(_rms_norm(dq, diff_qn_g[l]), pos)
        dk = _rope(_rms_norm(dk, diff_kn_g[l]), pos)
        lp = diff_lam[l].astype(jnp.float32)
        lam = jnp.exp(jnp.sum(lp[0] * lp[1])) - jnp.exp(jnp.sum(lp[2] * lp[3])) + lam_init
        o_b = _diff_attention(dq[0], dq[1], dk[0], dk[1], _heads(df_v), lam)
        o_b = _rms_norm(o_b, diff_subln_g[l]) * (1.0 - lam_init)

        mq = _rope(_rms_norm(_heads(mb_q), moba_qn_g[l]), pos)
        mk = _rope(_rms_norm(_heads(mb_k), moba_kn_g[l]), pos)
        o_c = _moba(mq, mk, _heads(mb_v))

        nq = _rope(_rms_norm(_heads(ns_q), nsa_qn_g[l]), pos)
        g_nsa = jax.nn.sigmoid(ns_g).reshape(b, s, 3, N_HEADS).transpose(2, 0, 3, 1)[..., None]
        o_d = _nsa(nq, ns_kc, ns_vc, ns_ks, ns_vs, ns_kw, ns_vw, g_nsa,
                   nsa_kn_g[l], nsa_cmp_pe[l], nsa_cmp_w[l])

        merged = None
        for i, o in enumerate((o_a, o_b, o_c, o_d)):
            g = jax.nn.sigmoid(xn @ w_gate[l, i] + b_gate[l, i])
            term = g * (_merge_heads(o) @ w_branch[l, i])
            merged = term if merged is None else merged + term
        x = x + merged @ w_out[l]

        hn = _rms_norm(x, ffn_norm_g[l])
        x = x + (jax.nn.silu(hn @ w_ffn_gate[l]) * (hn @ w_ffn_up[l])) @ w_ffn_down[l]
    return x


_drawn_inputs = setup_inputs


def setup_inputs(seed=0):
    import zlib

    import numpy as np

    out = dict(_drawn_inputs(seed))
    spreads = {}
    factors = {'moba_qn_g': 8.0, 'moba_kn_g': 8.0, 'nsa_qn_g': 6.484, 'nsa_kn_g': 7.597, 'b_gate': 8.0}
    for name, (base, spread) in spreads.items():
        noise = np.random.default_rng([zlib.crc32(name.encode()), seed]).standard_normal(out[name].shape)
        drawn = base * np.exp(spread * noise) if base else spread * noise
        out[name] = __import__('jax').numpy.asarray(drawn.astype(out[name].dtype))
    for name, factor in factors.items():
        out[name] = (out[name] * factor).astype(out[name].dtype)
    return out
```

```python
import math
from contextlib import ExitStack

import numpy as np

import concourse.bass as bass
from concourse import mybir

ALU = mybir.AluOpType
ACT = mybir.ActivationFunctionType
AX = mybir.AxisListType
F32 = mybir.dt.float32
F32R = mybir.dt.float32r
BF16 = mybir.dt.bfloat16

P = 128
SEQ, D_MODEL, DEPTH = 256, 1024, 2
NT = SEQ // P
KT = D_MODEL // P
H, HD = 4, 64
MIX = H * HD
DD = HD // 2
IN_COLS = 10 * MIX + 6 * HD + 3 * H
FFN = 2816
FC = 256
NC = 512
CMP_LEN, CMP_STRIDE, NCMP = 32, 16, 15
EPS = 1e-6
NEG = -1e30

SBQ, SBV, DFQ, DFK, DFV, MBQ, MBK, MBV, NSQ = (MIX * i for i in (0, 2, 3, 4, 5, 6, 7, 8, 9))
NKC = 10 * MIX
NKS, NVS, NKW, NVW, NGT = (NKC + HD * i for i in (2, 3, 4, 5, 6))

G_DQ, G_DK, G_MQ, G_MK, G_NQ, G_KC, G_KS, G_KW, G_SUB = 0, 32, 64, 128, 192, 256, 320, 384, 448

C_ID, C_TRI, C_ONE, C_R32, C_R64, C_CM, C_CZ, C_RC, C_REP, C_END = 0, 128, 256, 384, 416, 480, 512, 544, 576, 704

N_IN, N_GATE, N_FFN, N_DOWN = -(-IN_COLS // NC), 8, FFN // FC, FFN // P // 2
CHUNKS = ([("in", g, q) for g in range(N_IN) for q in range(4)]
          + [("gate", g, q) for g in range(N_GATE) for q in range(4)]
          + [("branch", i, c) for i in range(4) for c in range(2)]
          + [("out", q, c) for q in range(4) for c in range(2)]
          + [("ffn", j, q) for j in range(N_FFN) for q in range(4)]
          + [("down", 0, 1), ("down", 0, 0)]
          + [("down", j, c) for j in range(1, N_DOWN) for c in range(2)])
NCH = len(CHUNKS)
U_GATE, U_BR, U_OUT, U_FFN, U_DOWN = (next(n for n, c in enumerate(CHUNKS) if c[0] == k)
                                      for k in ("gate", "branch", "out", "ffn", "down"))
RAW, WR, LEAD = 4, 4, 2


def in_cols(g):
    return min(NC, IN_COLS - g * NC)


def steps():
    at = {u: [] for u in range(NCH + 2)}

    def put(u, *step):
        at[u].append(step)

    for kp, u in enumerate((0, 0, 1, 2)):
        put(u, "pair", ("x", kp))
        put(U_FFN + u, "pair", ("f", kp))
    for kp, u in enumerate((0, 1, 3, 5)):
        put(U_OUT + u, "pair", ("m", kp))
    put(1, "stats", "x")
    put(U_FFN + 1, "stats", "f")
    put(2, "lambda", None)
    for g in range(N_IN):
        put(4 * g + 4, "proj", g)
    put(6, "qk", "Aq")
    put(7, "qk", "Ak")
    for h in range(H):
        put(8 + 2 * h, "z", h)
        put(9 + 2 * h, "sp", h)
        put(10 + 2 * h, "cum", h)
        put(11 + 2 * h, "pv", ("A", h))
    put(18, "o", "A")
    put(20, "pair", ("o", 0))
    put(13, "prep", "B")
    put(19, "qk", "Bq")
    put(21, "qk", "Bk")
    for h in range(H):
        put(22 + 2 * h, "sm", ("B", h))
        put(23 + 2 * h, "p", ("B", h))
        put(25 + 2 * h, "pt", ("B", h))
        put(26 + 2 * h, "pv", ("B", h))
    put(33, "o", "B")
    put(34, "subln", None)
    put(42, "pair", ("o", 1))
    put(21, "prep", "C")
    put(30, "qk", "Cq")
    put(32, "qk", "Ck")
    for h in range(H):
        put(34 + h, "sm", ("C", h))
        put(35 + h, "p", ("C", h))
        put(37 + h, "pt", ("C", h))
        put(38 + h, "pv", ("C", h))
    put(42, "o", "C")
    put(52, "pair", ("o", 2))
    put(25, "prep", "D")
    put(26, "ngate", None)
    put(28, "qk", "Dc")
    put(29, "cbuild", None)
    put(31, "ck", None)
    put(32, "cv", None)
    put(33, "kcprep", None)
    put(33, "qk", "Dq")
    put(34, "qk", "Dk")
    put(35, "kct", None)
    put(36, "cr", None)
    put(38, "cs", None)
    put(40, "cp", None)
    put(41, "cpt", None)
    put(43, "cpv", None)
    for m in range(2 * H):
        put(40 + m, "sm", ("D", m))
        put(41 + m, "p", ("D", m))
        put(43 + m, "pt", ("D", m))
        put(44 + m, "pv", ("D", m))
    put(52, "o", "D")
    put(54, "pair", ("o", 3))
    for g in range(N_GATE):
        put(U_GATE + 4 * g + 4, "zg", g)
    for i, u in enumerate((52, 53, 55, 57)):
        put(u, "sig", i)
    for i in range(4):
        for c in range(2):
            put(U_BR + 2 * i + c + 1, "merge", (i, c))
    for c in range(2):
        put(U_OUT + 7 + c, "xadd", ("out", c))
        put(U_DOWN + 2 * N_DOWN - 1 + c, "xadd", ("down", c))
    for j in range(N_FFN):
        put(U_FFN + 4 * j + 4, "act", j)
        put(U_FFN + 4 * j + 5, "pair", ("h", j))
    return {u: sorted(s, key=rank) for u, s in at.items()}


def rank(step):
    kind, a = step
    if kind == "pair" and a[0] in "xfm":
        return 0 if a[1] == 0 else 2
    return 1 if kind in ("proj", "zg", "merge", "xadd", "act") else 3


STEPS = steps()


def steps_at(l, u):
    if u:
        return [(l, s) for s in STEPS[u]] if u < NCH or l == DEPTH - 1 else []
    late = [(l - 1, s) for s in STEPS[NCH]] if l else []
    return [(l, STEPS[0][0])] + late + [(l, s) for s in STEPS[0][1:]]


ORDER = [s for u in range(NCH + 1) for s in STEPS[u]]


def keys(*kinds):
    return [s for s in ORDER if s[0] in kinds]


class Events:

    def __init__(self, sem, order):
        self.sem, self.order, self.count = sem, order, 0
        self.place = {k: n for n, k in enumerate(order)}

    def at(self, layer, key):
        return layer * len(self.order) + self.place[key] + 1

    def now(self, key):
        assert self.order[self.count % len(self.order)] == key, (key, self.order[self.count % len(self.order)])
        self.count += 1
        return self.sem


TP, OB, S0, S1 = range(4)


def banks_of(step):
    kind, a = step
    if kind == "pair":
        if a[0] == "o":
            return (TP,)
        return ((S0, S1)[a[1] % 2],) if a[0] == "h" else ((TP, S0, S1, OB)[a[1]],)
    if kind in ("qk", "pt", "kct", "cpt", "cr"):
        return (TP,)
    if kind in ("z", "cum"):
        return ((S0, S1)[a % 2],)
    if kind == "sm":
        return (S0, S1) if a[0] == "B" else ((S0, S1)[a[1] % 2],)
    if kind == "cs":
        return (S0, S1)
    if kind == "ck":
        return (S0,)
    if kind == "cv":
        return (S1,)
    if kind == "o":
        return (OB,)
    return ()


def reader_of(step):
    return "dve" if step[0] in ("pair", "cs", "cv", "cr") else "act"


BANK_STEPS = [s for s in ORDER if banks_of(s)]
BANK_USES = {b: [s for s in BANK_STEPS if b in banks_of(s) and s[0] != "cum"] for b in range(4)}


def e_of(step):
    kind, a = step
    if kind == "z":
        return (2 * (a % 2), 2 * (a % 2) + 1), ("cum", a)
    if kind == "sm" and a[0] == "B":
        return (2 * (a[1] % 2), 2 * (a[1] % 2) + 1), ("pt", a)
    return (a[1] % 4,), ("pt", a)


E_STEPS = [s for s in ORDER if s[0] in ("z", "sm")]
PT_STEPS = [s for s in ORDER if s[0] in ("cum", "pt")]


def pv_step(s):
    return ("pv", ("A", s[1])) if s[0] == "cum" else ("pv", s[1])


def trunk_kernel(nc, x, w_in, w_gate, w_branch, w_out, w_ffn_gate, w_ffn_up, w_ffn_down,
                 norm_g, gains, lam, cmp_pe, cmp_w, b_gate, const, masks, out):
    with ExitStack() as ctx:
        def sem(name):
            return ctx.enter_context(nc.semaphore(name))

        base = nc.sbuf_base + (-nc.sbuf_base) % 64
        top = [base]

        def place(name, shape, dt, at=None):
            size = int(np.prod(shape[1:])) * (2 if dt == BF16 else 4)
            offset = top[0] if at is None else at
            if at is None:
                top[0] += size + (-size) % 32
            return nc.alloc_sbuf_tensor_at(name, shape, dt, offset=offset)

        w_raw = place("w_raw", [P, RAW, 2, NC], F32)
        w_hi = place("w_hi", [P, WR, 2, NC], F32R)
        w_lo = place("w_lo", [P, WR, 2, NC], F32R)
        xs = place("xs", [P, NT, D_MODEL], F32)
        xt_hi = place("xt_hi", [P, KT, SEQ], F32R)
        xt_lo = place("xt_lo", [P, KT, SEQ], F32R)
        ot_hi = place("ot_hi", [P, KT, SEQ], F32R)
        ot_lo = place("ot_lo", [P, KT, SEQ], F32R)
        big = top[0]
        proj = place("proj", [P, NT, IN_COLS], F32)
        zg = place("zg", [P, NT, 4, D_MODEL], F32)
        zg_at = big + NT * IN_COLS * 4
        zg_at += (-zg_at) % 32
        end_big = top[0]
        squares = place("squares", [P, NT, NC], F32, at=zg_at)
        merged = place("merged", [P, NT, D_MODEL], F32, at=big)
        prod = place("prod", [P, NT, D_MODEL], F32, at=big + 4 * NT * D_MODEL)
        ht_hi = place("ht_hi", [P, FFN // P, SEQ], F32R, at=big)
        ht_lo = place("ht_lo", [P, FFN // P, SEQ], F32R, at=big + 4 * FFN // P * SEQ)
        assert big + 8 * FFN // P * SEQ <= end_big
        osb = place("osb", [P, NT, D_MODEL], F32)
        bg = place("bg", [P, 2, D_MODEL], F32)
        big2 = top[0]
        cw = place("cw", [P, CMP_LEN, HD], F32)
        silu = place("silu", [P, NT, FC], F32, at=big2)
        hid = place("hid", [P, 2, NT, FC], F32, at=big2 + 4 * NT * FC)
        qk1 = place("qk1", [P, 4, SEQ], F32)
        qk2 = place("qk2", [P, 4, SEQ], F32)
        kcvt = place("kcvt", [P, SEQ], F32)
        eb = place("eb", [P, 4, 384], F32)
        ptb = place("ptb", [P, 2, 384], F32)
        ptc = place("ptc", [P, NT, P], F32)
        cblk = place("cblk", [P, CMP_LEN, 32], F32)
        vblk = place("vblk", [P, H, HD], F32)
        cst = place("cst", [P, C_END], F32)
        cst16 = place("cst16", [P, P + 2 * 384], BF16)
        gn = place("gn", [P, 512], F32)
        gt = place("gt", [P, 2 * KT], F32)
        pet = place("pet", [P, CMP_LEN], F32)
        lamb = place("lamb", [P, 4, DD], F32)
        rot_at = top[0]
        rot1 = place("rot1", [P, 256], F32)
        rot2 = place("rot2", [P, 256], F32)
        kdup = place("kdup", [P, NT, 4, HD], F32)
        kcs = place("kcs", [16, 2, HD], F32)
        csc = place("csc", [P, NT, H, 16], F32)
        cpb = place("cpb", [P, NT, H, 32], F32)
        vcs = place("vcs", [16, HD], F32)
        osq = place("osq", [P, NT, MIX], F32, at=rot_at)
        rot_l = place("rot_l", [P, 2 * DD], F32)
        small = place("small", [P, 256], F32)
        kcsq = place("kcsq", [16, 2, HD], F32)
        assert top[0] <= nc.sbuf_usable_end, top[0] - nc.sbuf_usable_end

        sm = lambda a, n: small[:, a:a + n]
        xss, xr = sm(0, 2), {"x": sm(2, 2), "f": sm(4, 2)}
        half = sm(8, 32)
        ss, rs = sm(40, 32), sm(72, 32)
        stat = [sm(104 + 4 * i, 4) for i in range(2)]
        nbias = [sm(112 + 4 * i, 4) for i in range(2)]
        sums = [sm(120 + 4 * i, 4) for i in range(2)]
        coef = [sm(128 + 4 * i, 4) for i in range(2)]
        ng = sm(136, 24)
        cmx, csum = sm(160, 8), sm(168, 8)
        nlam, lsum, lexp = sm(176, 1), sm(178, 2), sm(180, 2)
        kcss, kcr = small[0:16, 184:186], small[0:16, 186:188]
        obss = sm(190, 8)
        obr = sm(200, 8)
        xms = sm(210, 2)

        acc = [ctx.enter_context(nc.psum_tensor(f"acc{i}", [P, NC], F32)) for i in range(4)]
        att = ctx.enter_context(nc.psum_tensor("att", [P, 4, NC], F32))

        masks32 = eb[:, :, :].rearrange("p e n -> p (e n)")[:, 0:P + 2 * 384]
        ident, negtri, negone = cst[:, C_ID:C_ID + P], cst[:, C_TRI:C_TRI + P], cst[:, C_ONE:C_ONE + P]
        ident16, mask_a, mask_s = cst16[:, 0:P], cst16[:, P:P + 384], cst16[:, P + 384:P + 768]
        rope32 = cst[:, C_R32:C_R32 + 32].rearrange("p (t a r) -> p t a r", t=NT, a=2)
        rope64 = cst[:, C_R64:C_R64 + 64].rearrange("p (t a r) -> p t a r", t=NT, a=2)
        cmask = cst[:, C_CM:C_CM + 32].rearrange("p (t n) -> p t n", t=NT)
        czero = cst[:, C_CZ:C_CZ + 32].rearrange("p (t n) -> p t n", t=NT)
        ropec = cst[0:16, C_RC:C_RC + 32].rearrange("p (a r) -> p a r", a=2)

        s_const = sem("const_landed")
        s_mask = sem("masks_landed")
        s_mask16 = sem("masks_in_bf16")
        s_gt = sem("norm_gains_landed")
        s_x = sem("x_landed")
        s_raw = [sem(f"raw_landed{i}") for i in range(RAW)]
        s_small = sem("layer_params_landed")
        s_cw = sem("cmp_w_landed")
        s_bg = [sem(f"bias_landed{i}") for i in range(2)]
        s_out = sem("out_written")
        s_hi = sem("w_hi_ready")
        s_lo = sem("w_lo_ready")
        s_ch = sem("chunk_done")
        s_init = sem("buffers_cleared")

        att_keys = [s for s in ORDER if (banks_of(s) and s[0] != "o") or s[0] in ("pv", "cpv")]
        att_done = Events(sem("att_done"), att_keys)
        read_act = Events(sem("att_read_act"), [s for s in BANK_STEPS if reader_of(s) == "act" and s[0] != "z"])
        read_dve = Events(sem("att_read_dve"), [s for s in BANK_STEPS if reader_of(s) == "dve"])
        hi_done = Events(sem("pair_hi_done"), keys("pair"))
        proj_out = Events(sem("proj_read"), keys("proj"))
        act_misc = Events(sem("scalar_small"), [s for s in ORDER if s[0] in (
            "stats", "lambda", "prep", "ngate", "kcprep", "cs", "sig", "act")])
        dve_acc = Events(sem("acc_read_dve"), keys("zg", "merge", "xadd", "act"))
        dve_misc = Events(sem("vector_small"), [s for s in ORDER if s[0] in (
            "lambda", "prep", "ngate", "kcprep", "subln", "cbuild", "sm", "p", "sp", "cp")])
        merged_done = Events(sem("merged_done"), [s for s in keys("merge") if s[1][0] == 3])
        cs_exp = Events(sem("cs_max_done"), keys("cs"))
        cs_exp0 = Events(sem("lambda_sums"), keys("lambda"))
        s_zc = sem("softplus_chain")
        s_kd = sem("kdup_ready")
        s_dve = sem("vector_chain")
        s_pool = sem("gpsimd_chain")
        s_phalf = sem("exponent_set")
        sub_sq = Events(sem("subln_squares"), keys("subln"))
        pool_done = Events(sem("gpsimd_done"), [s for s in ORDER if s[0] in (
            "stats", "prep", "kcprep", "subln") or (s[0] == "merge" and s[1][0] in (1, 2))])

        def chunk(l, u):
            return l * NCH + u

        def weight(l, u):
            kind, a, b = CHUNKS[u]
            if kind == "in":
                n = in_cols(a)
                return [(w_in[l, 2 * b * P:(2 * b + 2) * P, a * NC:a * NC + n], slice(0, n))]
            if kind == "gate":
                return [(w_gate[l, a // 2, 2 * b * P:(2 * b + 2) * P, (a % 2) * NC:(a % 2 + 1) * NC], slice(0, NC))]
            if kind == "branch":
                return [(w_branch[l, a, :, b * NC:(b + 1) * NC], slice(0, NC))]
            if kind == "out":
                return [(w_out[l, 2 * a * P:(2 * a + 2) * P, b * NC:(b + 1) * NC], slice(0, NC))]
            if kind == "ffn":
                rows = slice(2 * b * P, (2 * b + 2) * P)
                return [(w_ffn_gate[l, rows, a * FC:(a + 1) * FC], slice(0, FC)),
                        (w_ffn_up[l, rows, a * FC:(a + 1) * FC], slice(FC, 2 * FC))]
            return [(w_ffn_down[l, 2 * a * P:(2 * a + 2) * P, b * NC:(b + 1) * NC], slice(0, NC))]

        def raw_value(n):
            return 16 * sum(2 if CHUNKS[m % NCH][0] == "ffn" else 1 for m in range(n % RAW, n + 1, RAW))

        def width(u):
            return in_cols(CHUNKS[u][1]) if CHUNKS[u][0] == "in" else NC

        def previous(l, uses, step):
            n = uses.index(step)
            return (l, uses[n - 1]) if n else ((l - 1, uses[-1]) if l else None)

        block = ctx.enter_context(nc.Block())

        @block.sync
        def _(sp):
            def load_chunk(n):
                l, u = divmod(n, NCH)
                if n >= RAW:
                    sp.wait_ge(s_lo, n - RAW + 1)
                for src, cols in weight(l, u):
                    sp.dma_start(w_raw[:, n % RAW, :, cols], src.rearrange("(k p) n -> p k n", p=P)
                                 ).then_inc(s_raw[n % RAW], 16)

            sp.dma_start(xs[:, :, :], x[0].rearrange("(t p) d -> p t d", p=P)).then_inc(s_x, 16)
            sp.dma_start(cst[:, :], const).then_inc(s_const, 16)
            sp.dma_start(gt[:, :], norm_g[0]).then_inc(s_gt, 16)
            for l in range(DEPTH):
                for u in range(NCH):
                    load_chunk(chunk(l, u))
                    if u == 1:
                        if l == 0:
                            sp.dma_start(masks32, masks).then_inc(s_mask, 16)
                        else:
                            sp.wait_ge(pool_done.sem, pool_done.at(l - 1, ("stats", "f")))
                        sp.dma_start(gn[:, :], gains[l].partition_broadcast(P)).then_inc(s_small, 16)
                        sp.dma_start(lamb[:, :, :], lam[l].partition_broadcast(P)).then_inc(s_small, 16)
                        sp.dma_start(pet[:, :], cmp_pe[l]).then_inc(s_small, 16)
                    if u == 3:
                        if l:
                            sp.wait_ge(att_done.sem, att_done.at(l - 1, ("pair", ("h", N_FFN - 1))))
                        sp.dma_start(cw[:, :, :], cmp_w[l]).then_inc(s_cw, 16)
                    if CHUNKS[u][0] == "gate" and CHUNKS[u][1] % 2 == 0 and CHUNKS[u][2] == 0:
                        i = CHUNKS[u][1] // 2
                        if i >= 2:
                            sp.wait_ge(dve_acc.sem, dve_acc.at(l, ("zg", 2 * i - 3)))
                        elif l:
                            sp.wait_ge(dve_acc.sem, dve_acc.at(l - 1, ("zg", 2 * i + 5)))
                        sp.dma_start(bg[:, i % 2, :], b_gate[l, i].partition_broadcast(P)
                                     ).then_inc(s_bg[i % 2], 16)
                    if u == U_FFN + 6 and l + 1 < DEPTH:
                        sp.wait_ge(read_dve.sem, read_dve.at(l, ("pair", ("f", KT // 2 - 1))))
                        sp.dma_start(gt[:, :], norm_g[l + 1]).then_inc(s_gt, 16)
            for c in range(2):
                sp.wait_ge(dve_acc.sem, dve_acc.at(DEPTH - 1, ("xadd", ("down", c))))
                sp.dma_start(out[0, :, c * NC:(c + 1) * NC].rearrange("(t p) d -> p t d", p=P),
                             xs[:, :, c * NC:(c + 1) * NC]).then_inc(s_out, 16)
            sp.wait_ge(s_out, 32)

        @block.tensor
        def _(pe):
            def bank_free(l, step):
                for b in banks_of(step):
                    prev = previous(l, BANK_USES[b], step)
                    if prev:
                        before = ("cum", prev[1][1]) if prev[1][0] == "z" else prev[1]
                        ev = read_dve if reader_of(before) == "dve" else read_act
                        pe.wait_ge(ev.sem, ev.at(prev[0], before))

            def products(l, u):
                kind, a, b = CHUNKS[u]
                n = chunk(l, u)
                pe.wait_ge(s_lo, n + 1)
                N = width(u)
                first, last = {"in": (b == 0, b == 3), "gate": (b == 0, b == 3), "branch": (True, True),
                               "out": (a == 0, a == 3), "ffn": (b == 0, b == 3),
                               "down": (a == 0, a == N_DOWN - 1)}[kind]
                hi, lo, k0 = {"branch": (ot_hi, ot_lo, 2 * a), "out": (xt_hi, xt_lo, 2 * a),
                              "down": (ht_hi, ht_lo, 2 * a)}.get(kind, (xt_hi, xt_lo, 2 * b))
                src = {"in": ("x", b) if a == 0 else None, "ffn": ("f", b) if a == 0 else None, "gate": None,
                       "branch": ("o", a), "out": ("m", a), "down": ("h", a)}[kind]
                if src:
                    pe.wait_ge(hi_done.sem, hi_done.at(l, ("pair", src)))
                if first:
                    if kind == "in" and a >= 2:
                        pe.wait_ge(proj_out.sem, proj_out.at(l, ("proj", a - 2)))
                    elif kind == "in" and l:
                        pe.wait_ge(dve_acc.sem, dve_acc.at(l - 1, ("xadd", ("down", a))))
                    elif kind == "gate" and a < 2:
                        pe.wait_ge(proj_out.sem, proj_out.at(l, ("proj", N_IN - 2 + a)))
                    elif kind == "gate":
                        pe.wait_ge(dve_acc.sem, dve_acc.at(l, ("zg", a - 2)))
                    elif kind == "branch":
                        pe.wait_ge(dve_acc.sem, dve_acc.at(l, ("merge", (a - 1, b)) if a else ("zg", N_GATE - 2 + b)))
                    elif kind == "out":
                        pe.wait_ge(dve_acc.sem, dve_acc.at(l, ("merge", (3, b))))
                    elif kind == "ffn":
                        pe.wait_ge(dve_acc.sem, dve_acc.at(l, ("act", a - 2) if a >= 2 else ("xadd", ("out", a))))
                    elif kind == "down":
                        pe.wait_ge(dve_acc.sem, dve_acc.at(l, ("act", N_FFN - 1 - (b + N_FFN - 1) % 2)))
                pair = 2 * (a % 2) if kind in ("in", "gate", "ffn") else 2 * b
                wh = w_hi[:, n % WR, :, :]
                wl = w_lo[:, n % WR, :, :]
                for t in range(NT):
                    for k in range(2):
                        x_hi = hi[:, k0 + k, t * P:(t + 1) * P]
                        pe.matmul(acc[pair + t][:, 0:N], x_hi, wh[:, k, 0:N], start=first and k == 0, stop=False)
                        pe.matmul(acc[pair + t][:, 0:N], x_hi, wl[:, k, 0:N], start=False, stop=False)
                if src:
                    pe.wait_ge(read_dve.sem, read_dve.at(l, ("pair", src)))
                for t in range(NT):
                    for k in range(2):
                        last_mm = pe.matmul(acc[pair + t][:, 0:N], lo[:, k0 + k, t * P:(t + 1) * P], wh[:, k, 0:N],
                                            start=False, stop=last and k == 1)
                last_mm.then_inc(s_ch, 1)

            def pair(l, step):
                (what, kp), b = step[1], banks_of(step)[0]
                bank_free(l, step)
                if what == "x":
                    if l:
                        pe.wait_ge(dve_acc.sem, dve_acc.at(l - 1, ("xadd", ("down", kp // 2))))
                    elif kp == 0:
                        pe.wait_ge(s_x, 16)
                        pe.wait_ge(s_const, 16)
                if what == "f":
                    pe.wait_ge(dve_acc.sem, dve_acc.at(l, ("xadd", ("out", kp // 2))))
                if what == "m":
                    pe.wait_ge(merged_done.sem, merged_done.at(l, ("merge", (3, kp // 2))))
                if what == "o":
                    pe.wait_ge(read_act.sem, read_act.at(l, ("o", "ABCD"[kp])))
                    if kp == 1:
                        pe.wait_ge(pool_done.sem, pool_done.at(l, ("subln", None)))
                if what == "h":
                    pe.wait_ge(dve_acc.sem, dve_acc.at(l, ("act", kp)))
                for k in range(2):
                    for t in range(NT):
                        col = slice((2 * kp + k) * P, (2 * kp + k + 1) * P)
                        src = {"x": xs, "f": xs, "m": merged, "o": osb}.get(what)
                        src = hid[:, kp % 2, t, k * P:(k + 1) * P] if what == "h" else src[:, t, col]
                        mm = pe.transpose(att[:, b, (2 * k + t) * P:(2 * k + t + 1) * P], src, ident)
                mm.then_inc(att_done.now(step), 1)

            def qk(l, step):
                name = step[1]
                bank_free(l, step)
                if name[0] == "A":
                    pe.wait_ge(proj_out.sem, proj_out.at(l, ("proj", 0)))
                elif name == "Dc":
                    pe.wait_ge(proj_out.sem, proj_out.at(l, ("proj", N_IN - 1)))
                else:
                    pe.wait_ge(pool_done.sem, pool_done.at(l, ("prep", name[0])))
                c0 = {"Aq": SBQ, "Ak": SBQ + MIX, "Bq": DFQ, "Bk": DFK, "Cq": MBQ, "Ck": MBK,
                      "Dq": NSQ, "Dc": NKC}.get(name)
                for m in range(1 if name == "Dc" else 2):
                    for t in range(NT):
                        src = (kdup[:, t, 2 * m:2 * m + 2, :] if name == "Dk"
                               else proj[:, t, c0 + m * P:c0 + (m + 1) * P])
                        mm = pe.transpose(att[:, TP, (2 * m + t) * P:(2 * m + t + 1) * P], src, ident)
                mm.then_inc(att_done.now(step), 1)

            def causal(b, mask, q, k, swap=False):
                pe.matmul(att[:, b, 0:384], ident16, mask, start=True, stop=False, skip_group_check=True)
                if swap:
                    pe.matmul(att[:, b, 0:256], k[:, 0:P], q[:, 0:256], start=False, stop=False,
                              skip_group_check=True)
                    return pe.matmul(att[:, b, 256:384], k[:, P:2 * P], q[:, P:2 * P], start=False,
                                     stop=True, skip_group_check=True)
                pe.matmul(att[:, b, 0:P], q[:, 0:P], k[:, 0:P], start=False, stop=False,
                          skip_group_check=True)
                return pe.matmul(att[:, b, P:384], q[:, P:2 * P], k[:, 0:256], start=False, stop=True,
                                 skip_group_check=True)

            def scores(l, step):
                kind, a = step
                bank_free(l, step)
                if kind == "z":
                    r = slice(64 * (a % 2), 64 * (a % 2) + 64)
                    if a == 0:
                        pe.wait_ge(read_act.sem, read_act.at(l, ("qk", "Ak")))
                        if l == 0:
                            pe.wait_ge(s_mask16, 1)
                    mm = causal(S0 + a % 2, mask_a, qk1[r, a // 2, :], qk1[r, 2 + a // 2, :], swap=True)
                    mm.then_inc(att_done.now(step), 1)
                    return
                mixer, h = a
                if h == 0:
                    pe.wait_ge(read_act.sem, read_act.at(l, ("qk", mixer + "k")))
                if mixer == "B":
                    for m in range(2):
                        r = slice(64 * (h % 2) + 32 * m, 64 * (h % 2) + 32 * m + 32)
                        mm = causal(S0 + m, mask_s, qk2[r, h // 2, :], qk2[r, 2 + h // 2, :])
                elif mixer == "C":
                    r = slice(64 * (h % 2), 64 * (h % 2) + 64)
                    mm = causal(S0 + h % 2, mask_s, qk1[r, h // 2, :], qk1[r, 2 + h // 2, :])
                else:
                    m, h = h % 2, h // 2
                    r = slice(64 * (h % 2), 64 * (h % 2) + 64)
                    mm = causal(S0 + m, mask_s, qk2[r, h // 2, :], qk2[r, 2 + m, :])
                mm.then_inc(att_done.now(step), 1)

            def cumulate(l, step):
                h = step[1]
                b = S0 + h % 2
                sp_t = eb[:, 2 * (h % 2) + 1, :]
                pe.wait_ge(dve_misc.sem, dve_misc.at(l, ("sp", h)))
                pe.matmul(att[:, b, 0:384], negtri, sp_t, start=False, stop=False, skip_group_check=True)
                pe.matmul(att[:, b, P:2 * P], negone, sp_t[:, 256:384], start=False, stop=True,
                          skip_group_check=True).then_inc(att_done.now(step), 1)

            def transpose_p(l, step):
                bank_free(l, step)
                if step[0] == "cpt":
                    pe.wait_ge(dve_misc.sem, dve_misc.at(l, ("cp", None)))
                    for t in range(NT):
                        mm = pe.transpose(att[:, TP, t * P:(t + 1) * P], cpb[:, t, :, :], ident)
                else:
                    mixer, m = step[1]
                    e = 2 * (m % 2) if mixer == "B" else m % 4
                    pe.wait_ge(dve_misc.sem, dve_misc.at(l, ("p", step[1])))
                    for s in range(3):
                        mm = pe.transpose(att[:, TP, s * P:(s + 1) * P], eb[:, e, s * P:(s + 1) * P], ident)
                mm.then_inc(att_done.now(step), 1)

            def times_v(l, step):
                mixer, m = step[1]
                src = ("cum", m) if mixer == "A" else ("pt", (mixer, m))
                pe.wait_ge(read_act.sem, read_act.at(l, src))
                pb = PT_STEPS.index(src) % 2
                h = m // 2 if mixer == "D" else m
                v0 = {"A": SBV + h * HD, "B": DFV + h * HD, "C": MBV + h * HD}.get(mixer, (NVS, NVW)[m % 2])
                if mixer == "A":
                    pe.wait_ge(proj_out.sem, proj_out.at(l, ("proj", 1)))
                if m == 0 and mixer != "D":
                    bank_free(l, ("o", mixer))
                own = mixer != "D"
                for t in range(NT):
                    dst = att[:, OB, t * MIX + h * HD:t * MIX + (h + 1) * HD]
                    for s in range(t + 1):
                        mm = pe.matmul(dst, ptb[:, pb, (t + s) * P:(t + s + 1) * P], proj[:, s, v0:v0 + HD],
                                       start=own and s == 0, stop=s == t, skip_group_check=True)
                mm.then_inc(att_done.now(step), 1)

            def compress(l, step):
                bank_free(l, step)
                pe.wait_ge(dve_misc.sem, dve_misc.at(l, ("cbuild", None)))
                pe.wait_ge(s_cw, 16 * (l + 1))
                for j in range(CMP_LEN):
                    b, r = (S0, slice(0, 64)) if step[0] == "ck" else (S1, slice(64, 128))
                    mm = pe.matmul(att[0:16, b, 0:HD], cblk[r, j, 0:16], cw[r, j, :],
                                   start=j == 0, stop=j == CMP_LEN - 1)
                mm.then_inc(att_done.now(step), 1)

            for l in range(DEPTH):
                for u in range(NCH):
                    for step in STEPS[u]:
                        kind, a = step
                        if kind == "pair":
                            pair(l, step)
                        elif kind == "qk":
                            qk(l, step)
                        elif kind in ("z", "sm"):
                            scores(l, step)
                        elif kind == "cum":
                            cumulate(l, step)
                        elif kind in ("pt", "cpt"):
                            transpose_p(l, step)
                        elif kind == "pv":
                            times_v(l, step)
                        elif kind in ("ck", "cv"):
                            compress(l, step)
                        elif kind == "cr":
                            bank_free(l, step)
                            pe.wait_ge(read_dve.sem, read_dve.at(l, ("cv", None)))
                            pe.matmul(att[:, TP, 0:HD], cst[0:16, C_REP:C_REP + P], vcs[:, :], start=True, stop=True
                                      ).then_inc(att_done.now(step), 1)
                        elif kind == "kct":
                            bank_free(l, step)
                            pe.wait_ge(pool_done.sem, pool_done.at(l, ("kcprep", None)))
                            pe.transpose(att[:, TP, 0:16], kcs[:, :, :], ident[0:16, 0:16]
                                         ).then_inc(att_done.now(step), 1)
                        elif kind == "cs":
                            bank_free(l, step)
                            pe.wait_ge(read_act.sem, read_act.at(l, ("kct", None)))
                            for h in range(H):
                                r = slice(64 * (h % 2), 64 * (h % 2) + 64)
                                for t in range(NT):
                                    at = (2 * t + h // 2) * 16
                                    mm = pe.matmul(att[:, S0 + h % 2, at:at + 16], qk2[r, h // 2, t * P:(t + 1) * P],
                                                   kcvt[r, 0:16], start=True, stop=True)
                            mm.then_inc(att_done.now(step), 1)
                        elif kind == "cpv":
                            bank_free(l, ("o", "D"))
                            pe.wait_ge(read_act.sem, read_act.at(l, ("cpt", None)))
                            pe.wait_ge(read_dve.sem, read_dve.at(l, ("cr", None)))
                            for t in range(NT):
                                mm = pe.matmul(att[:, OB, t * MIX:(t + 1) * MIX], ptc[:, t, :], vblk[:, :, :],
                                               start=t == 0, stop=True, skip_group_check=True)
                            mm.then_inc(att_done.now(step), 1)
                    products(l, u)

        @block.scalar
        def _(act):
            copy = ACT.Copy

            def split(n):
                if n >= DEPTH * NCH:
                    return
                if n >= WR:
                    act.wait_ge(s_ch, n - WR + 1)
                act.wait_ge(s_raw[n % RAW], raw_value(n))
                N = width(n % NCH)
                act.activation(w_hi[:, n % WR, :, 0:N], w_raw[:, n % RAW, :, 0:N], copy).then_inc(s_hi, 1)

            def pair_hi(l, step):
                (what, kp), b = step[1], banks_of(step)[0]
                act.wait_ge(att_done.sem, att_done.at(l, step))
                if what in "xm" or what == "f":
                    n = chunk(l, {"x": 0, "m": U_OUT, "f": U_FFN}[what])
                    if n:
                        act.wait_ge(s_ch, n)
                dst = {"o": ot_hi, "h": ht_hi}.get(what, xt_hi)
                if what in "xf":
                    if l == 0 or what == "x":
                        act.wait_ge(s_gt, 16 * (l + 1))
                    for k in range(2):
                        g = gt[:, 2 * kp + k + (KT if what == "f" else 0):][:, 0:1]
                        ins = act.activation(dst[:, 2 * kp + k, :], att[:, b, k * SEQ:(k + 1) * SEQ], copy, scale=g)
                else:
                    ins = act.activation(dst[:, 2 * kp:2 * kp + 2, :].rearrange("p k t -> p (k t)"), att[:, b, :], copy)
                ins.then_inc(hi_done.now(step), 1)

            def qk_copy(l, step):
                name = step[1]
                act.wait_ge(att_done.sem, att_done.at(l, step))
                if name == "Dc":
                    if l:
                        act.wait_ge(att_done.sem, att_done.at(l - 1, ("cs", None)))
                    act.activation(kcvt[:, :], att[:, TP, 0:SEQ], copy).then_inc(read_act.now(step), 1)
                    return
                dst = (qk1 if name[0] in "AC" else qk2)[:, 0 if name[1] == "q" else 2:][:, 0:2, :]
                act.activation(dst.rearrange("p m t -> p (m t)"), att[:, TP, :], copy,
                               scale=HD ** -0.5 if name == "Aq" else 1.0).then_inc(read_act.now(step), 1)

            def e_free(l, step):
                mine = e_of(step)[0]
                uses = [s for s in E_STEPS if set(e_of(s)[0]) & set(mine)]
                for e in mine:
                    prev = previous(l, [s for s in uses if e in e_of(s)[0]], step)
                    if prev:
                        act.wait_ge(att_done.sem, att_done.at(prev[0], e_of(prev[1])[1]))

            def pt_free(l, step):
                n = l * len(PT_STEPS) + PT_STEPS.index(step) - 2
                if n >= 0:
                    act.wait_ge(att_done.sem, att_done.at(n // len(PT_STEPS), pv_step(PT_STEPS[n % len(PT_STEPS)])))
                return PT_STEPS.index(step) % 2

            def exps(l, step):
                mixer, m = step[1]
                scale = (DD if mixer == "B" else HD) ** -0.5
                r = keys("sm").index(step) % 2
                act.wait_ge(att_done.sem, att_done.at(l, step))
                act.wait_ge(dve_misc.sem, dve_misc.at(l, step))
                e_free(l, step)
                maps = 2 if mixer == "B" else 1
                for i in range(maps):
                    b = banks_of(step)[i]
                    e = e_of(step)[0][i]
                    for t, cols in enumerate((slice(0, P), slice(P, 384))):
                        j = maps * t + i
                        ins = act.activation(eb[:, e, cols], att[:, b, cols], ACT.Exp, scale=scale,
                                             bias=nbias[r][:, j:j + 1], accum_out=sums[r][:, j:j + 1])
                ins.then_inc(read_act.now(step), 1)

            ev = [0]

            def do(l, step):
                kind, a = step
                if kind == "proj":
                    act.wait_ge(s_ch, chunk(l, 4 * a + 4))
                    if a == 0:
                        act.wait_ge(pool_done.sem, pool_done.at(l, ("stats", "x")))
                    N = in_cols(a)
                    for t in range(NT):
                        ins = act.activation(proj[:, t, a * NC:a * NC + N], acc[2 * (a % 2) + t][:, 0:N],
                                             copy, scale=xr["x"][:, t:t + 1])
                    ins.then_inc(proj_out.now(step), 1)
                elif kind == "act":
                    act.wait_ge(s_ch, chunk(l, U_FFN + 4 * a + 4))
                    if a == 0:
                        act.wait_ge(pool_done.sem, pool_done.at(l, ("stats", "f")))
                    else:
                        act.wait_ge(dve_acc.sem, dve_acc.at(l, ("act", a - 1)))
                    for t in range(NT):
                        ins = act.activation(silu[:, t, :], acc[2 * (a % 2) + t][:, 0:FC], ACT.Silu,
                                             scale=xr["f"][:, t:t + 1])
                    ins.then_inc(act_misc.now(step), 1)
                elif kind == "pair":
                    pair_hi(l, step)
                elif kind == "stats":
                    if a == "x" and l == 0:
                        act.wait_ge(s_x, 16)
                    else:
                        prev = (l - 1, ("xadd", ("down", 1))) if a == "x" else (l, ("xadd", ("out", 1)))
                        act.wait_ge(dve_acc.sem, dve_acc.at(*prev))
                    for t in range(NT):
                        ins = act.activation(osb[:, t, :], xs[:, t, :], ACT.Square, accum_out=xss[:, t:t + 1])
                    ins.then_inc(act_misc.now(step), 1)
                elif kind == "lambda":
                    act.wait_ge(cs_exp0.sem, cs_exp0.at(l, step))
                    act.activation(lexp, lsum, ACT.Exp).then_inc(act_misc.now(step), 1)
                elif kind == "qk":
                    qk_copy(l, step)
                elif kind == "z":
                    act.wait_ge(att_done.sem, att_done.at(l, step))
                    e_free(l, step)
                    t1 = eb[:, 2 * (a % 2), :]
                    for f, kw in ((ACT.Abs, {}), (ACT.Exp, {"scale": -1.0}), (ACT.Ln, {"bias": 1.0})):
                        ins = act.activation(t1, att[:, S0 + a % 2, 0:384] if f == ACT.Abs else t1, f, **kw)
                        ins.then_inc(s_zc, 1)
                        ev[0] += 1
                        if f != ACT.Ln:
                            act.wait_ge(s_zc, ev[0])
                elif kind == "cum":
                    act.wait_ge(att_done.sem, att_done.at(l, step))
                    pb = pt_free(l, step)
                    act.activation(ptb[:, pb, :], att[:, S0 + a % 2, 0:384], ACT.Exp
                                   ).then_inc(read_act.now(step), 1)
                elif kind == "sm":
                    exps(l, step)
                elif kind == "pt":
                    act.wait_ge(att_done.sem, att_done.at(l, step))
                    pb = pt_free(l, step)
                    act.activation(ptb[:, pb, :], att[:, TP, 0:384], copy).then_inc(read_act.now(step), 1)
                elif kind == "cpt":
                    act.wait_ge(att_done.sem, att_done.at(l, step))
                    if l:
                        act.wait_ge(att_done.sem, att_done.at(l - 1, ("cpv", None)))
                    act.activation(ptc[:, :, :].rearrange("p t q -> p (t q)"), att[:, TP, 0:SEQ], copy
                                   ).then_inc(read_act.now(step), 1)
                elif kind == "o":
                    last = {"D": 2 * H - 1}.get(a, H - 1)
                    act.wait_ge(att_done.sem, att_done.at(l, ("pv", (a, last))))
                    i = "ABCD".index(a)
                    act.activation(osb[:, :, i * MIX:(i + 1) * MIX],
                                   att[:, OB, :].rearrange("p (t d) -> p t d", t=NT), copy
                                   ).then_inc(read_act.now(step), 1)
                elif kind == "prep":
                    act.wait_ge(proj_out.sem, proj_out.at(l, ("proj", {"B": 2, "C": 3, "D": 5}[a])))
                    if a != "B":
                        act.wait_ge(dve_misc.sem, dve_misc.at(l, ("prep", {"C": "B", "D": "C"}[a])))
                    if a == "D":
                        for m, c in ((0, NKS), (1, NKS), (2, NKW), (3, NKW)):
                            act.activation(kdup[:, :, m, :], proj[:, :, c:c + HD], copy)
                        act.activation(squares[:, :, 0:MIX], proj[:, :, NSQ:NSQ + MIX], ACT.Square
                                       ).then_inc(s_kd, 1)
                        act.wait_ge(s_kd, l + 1)
                        act.activation(squares[:, :, MIX:2 * MIX], kdup[:, :, :, :].rearrange("p t m d -> p t (m d)"),
                                       ACT.Square).then_inc(act_misc.now(step), 1)
                    else:
                        c0 = DFQ if a == "B" else MBQ
                        act.activation(squares[:, :, :], proj[:, :, c0:c0 + 2 * MIX], ACT.Square
                                       ).then_inc(act_misc.now(step), 1)
                elif kind == "ngate":
                    act.activation(ng.rearrange("p (t g) -> p t g", t=NT), proj[:, :, NGT:NGT + 3 * H], ACT.Exp,
                                   scale=-1.0).then_inc(act_misc.now(step), 1)
                elif kind == "ck":
                    act.wait_ge(att_done.sem, att_done.at(l, step))
                    for m in range(2):
                        ins = act.activation(kcs[:, m, :], att[0:16, S0, 0:HD], copy)
                    ins.then_inc(read_act.now(step), 1)
                elif kind == "kcprep":
                    act.wait_ge(read_act.sem, read_act.at(l, ("ck", None)))
                    act.activation(kcsq[:, :, :], kcs[:, :, :], ACT.Square).then_inc(act_misc.now(step), 1)
                elif kind == "kct":
                    act.wait_ge(att_done.sem, att_done.at(l, step))
                    act.activation(kcvt[:, 0:16], att[:, TP, 0:16], copy).then_inc(read_act.now(step), 1)
                elif kind == "cs":
                    act.wait_ge(cs_exp.sem, cs_exp.at(l, step))
                    act.activation(csc[:, :, :, :].rearrange("p t h n -> p (t h n)"),
                                   csc[:, :, :, :].rearrange("p t h n -> p (t h n)"), ACT.Exp, scale=HD ** -0.5
                                   ).then_inc(act_misc.now(step), 1)
                elif kind == "sig":
                    act.wait_ge(dve_acc.sem, dve_acc.at(l, ("zg", 2 * a + 1)))
                    act.activation(zg[:, :, a, :], zg[:, :, a, :], ACT.Sigmoid).then_inc(act_misc.now(step), 1)

            for l in range(DEPTH):
                for u in range(NCH + 1):
                    todo = steps_at(l, u)
                    for n, (ll, step) in enumerate(todo):
                        if rank(step) < 3:
                            do(ll, step)
                        if l == u == 0 and n < LEAD:
                            split(n)
                    if u == NCH:
                        continue
                    split(chunk(l, u) + LEAD)
                    if l == 0 and u == 3:
                        act.wait_ge(s_mask, 16)
                        act.activation(cst16[:, :], masks32, copy).then_inc(s_mask16, 1)
                    for ll, step in todo:
                        if rank(step) == 3:
                            do(ll, step)

        @block.vector
        def _(dve):
            chain = [0]

            def settled(ins):
                ins.then_inc(s_dve, 1)
                chain[0] += 1
                dve.wait_ge(s_dve, chain[0])

            def split(n):
                if n >= DEPTH * NCH:
                    return
                dve.wait_ge(s_hi, n + 1)
                N = width(n % NCH)
                dve.tensor_tensor(w_lo[:, n % WR, :, 0:N], w_raw[:, n % RAW, :, 0:N],
                                  w_hi[:, n % WR, :, 0:N].bitcast(F32), ALU.subtract).then_inc(s_lo, 1)

            def pair_lo(l, step):
                (what, kp), b = step[1], banks_of(step)[0]
                dve.wait_ge(hi_done.sem, hi_done.at(l, step))
                hi, lo = {"o": (ot_hi, ot_lo), "h": (ht_hi, ht_lo)}.get(what, (xt_hi, xt_lo))
                if what in "xf":
                    for k in range(2):
                        g = gt[:, 2 * kp + k + (KT if what == "f" else 0):][:, 0:1]
                        ins = dve.scalar_tensor_tensor(out=lo[:, 2 * kp + k, :], in0=att[:, b, k * SEQ:(k + 1) * SEQ],
                                                       scalar=g, in1=hi[:, 2 * kp + k, :].bitcast(F32),
                                                       op0=ALU.mult, op1=ALU.subtract)
                else:
                    ins = dve.tensor_tensor(lo[:, 2 * kp:2 * kp + 2, :].rearrange("p k t -> p (k t)"), att[:, b, :],
                                            hi[:, 2 * kp:2 * kp + 2, :].rearrange("p k t -> p (k t)").bitcast(F32),
                                            ALU.subtract)
                ins.then_inc(read_dve.now(step), 1)

            dve.memset(cblk[:, :, :], 0.0).then_inc(s_init, 1)
            dve.memset(vblk[:, :, :], 0.0).then_inc(s_init, 1)
            dve.memset(cpb[:, :, :, :], 0.0).then_inc(s_init, 1)
            dve.wait_ge(s_init, 3)
            def do(l, step):
                kind, a = step
                if kind == "zg":
                    dve.wait_ge(s_ch, chunk(l, U_GATE + 4 * a + 4))
                    i, c = divmod(a, 2)
                    dve.wait_ge(s_bg[i % 2], 16 * (2 * l + i // 2 + 1))
                    for t in range(NT):
                        ins = dve.scalar_tensor_tensor(
                            out=zg[:, t, i, c * NC:(c + 1) * NC], in0=acc[2 * (a % 2) + t][:, :],
                            scalar=xr["x"][:, t:t + 1], in1=bg[:, i % 2, c * NC:(c + 1) * NC],
                            op0=ALU.mult, op1=ALU.add)
                    ins.then_inc(dve_acc.now(step), 1)
                elif kind == "merge":
                    i, c = a
                    dve.wait_ge(s_ch, chunk(l, U_BR + 2 * i + c + 1))
                    dve.wait_ge(act_misc.sem, act_misc.at(l, ("sig", i)))
                    cols = slice(c * NC, (c + 1) * NC)
                    if i >= 2:
                        dve.wait_ge(pool_done.sem, pool_done.at(l, ("merge", (i - 1, c))))
                    dst = merged if i == 0 else prod
                    for t in range(NT):
                        ins = dve.tensor_tensor(dst[:, t, cols], acc[2 * c + t][:, :], zg[:, t, i, cols], ALU.mult)
                    ins.then_inc(dve_acc.now(step), 1)
                    if i == 3:
                        dve.wait_ge(dve_acc.sem, dve_acc.at(l, step))
                        for t in range(NT):
                            ins = dve.tensor_tensor(merged[:, t, cols], merged[:, t, cols], prod[:, t, cols], ALU.add)
                        ins.then_inc(merged_done.now(step), 1)
                elif kind == "xadd":
                    what, c = a
                    dve.wait_ge(s_ch, chunk(l, (U_OUT + 6 if what == "out" else U_DOWN + 2 * N_DOWN - 2) + c + 1))
                    cols = slice(c * NC, (c + 1) * NC)
                    for t in range(NT):
                        ins = dve.tensor_tensor(xs[:, t, cols], acc[2 * c + t][:, :], xs[:, t, cols], ALU.add)
                    ins.then_inc(dve_acc.now(step), 1)
                elif kind == "act":
                    dve.wait_ge(act_misc.sem, act_misc.at(l, step))
                    if a >= 2:
                        dve.wait_ge(att_done.sem, att_done.at(l, ("pair", ("h", a - 2))))
                    for t in range(NT):
                        ins = dve.scalar_tensor_tensor(
                            out=hid[:, a % 2, t, :], in0=acc[2 * (a % 2) + t][:, FC:2 * FC],
                            scalar=xr["f"][:, t:t + 1], in1=silu[:, t, :], op0=ALU.mult, op1=ALU.mult)
                    ins.then_inc(dve_acc.now(step), 1)
                elif kind == "pair":
                    pair_lo(l, step)
                elif kind == "lambda":
                    dve.wait_ge(s_small, 48 * (l + 1))
                    lv = lamb[:, :, :].rearrange("p (a b) d -> p a b d", b=2)
                    lp = rot_l[:, :].rearrange("p (a d) -> p a d", a=2)
                    settled(dve.tensor_tensor(lp, lv[:, :, 0, :], lv[:, :, 1, :], ALU.mult))
                    dve.tensor_reduce(lsum, lp, AX.X, ALU.add).then_inc(cs_exp0.now(step), 1)
                    dve.wait_ge(act_misc.sem, act_misc.at(l, step))
                    settled(dve.tensor_tensor(nlam, lexp[:, 1:2], lexp[:, 0:1], ALU.subtract))
                    dve.tensor_scalar(nlam, nlam, -lam_init(l), None, ALU.add).then_inc(dve_misc.now(step), 1)
                elif kind == "prep":
                    dve.wait_ge(act_misc.sem, act_misc.at(l, step))
                    d = DD if a == "B" else HD
                    n = NT * 2 * MIX // d
                    prev = {"B": ("prep", "D"), "C": ("prep", "B"), "D": ("prep", "C")}[a]
                    if l or a != "B":
                        dve.wait_ge(pool_done.sem, pool_done.at(l - (a == "B"), prev))
                    dve.tensor_reduce(ss[:, 0:n], squares[:, :, :].rearrange("p t (u d) -> p (t u) d", d=d),
                                      AX.X, ALU.add).then_inc(dve_misc.now(step), 1)
                elif kind == "kcprep":
                    dve.wait_ge(act_misc.sem, act_misc.at(l, step))
                    dve.tensor_reduce(kcss, kcsq[:, :, :], AX.X, ALU.add).then_inc(dve_misc.now(step), 1)
                elif kind == "subln":
                    dve.wait_ge(sub_sq.sem, sub_sq.at(l, step))
                    dve.tensor_reduce(obss, osq[:, :, :].rearrange("p t (h d) -> p (t h) d", d=HD),
                                      AX.X, ALU.add).then_inc(dve_misc.now(step), 1)
                elif kind == "sp":
                    dve.wait_ge(s_zc, 3 * (l * H + a + 1))
                    dve.scalar_tensor_tensor(out=eb[:, 2 * (a % 2) + 1, :], in0=att[:, S0 + a % 2, 0:384], scalar=0.0,
                                             in1=eb[:, 2 * (a % 2), :], op0=ALU.max, op1=ALU.add
                                             ).then_inc(dve_misc.now(step), 1)
                elif kind == "sm":
                    mixer, m = a
                    r = keys("sm").index(step) % 2
                    b, maps = banks_of(step)[0], len(banks_of(step))
                    dve.wait_ge(att_done.sem, att_done.at(l, step))
                    dve.tensor_reduce(stat[r][:, 0:maps], att[:, b:b + maps, 0:P], AX.X, ALU.max)
                    settled(dve.tensor_reduce(stat[r][:, maps:2 * maps], att[:, b:b + maps, P:384], AX.X, ALU.max))
                    dve.tensor_scalar(nbias[r][:, 0:2 * maps], stat[r][:, 0:2 * maps],
                                      -(DD if mixer == "B" else HD) ** -0.5, None, ALU.mult
                                      ).then_inc(dve_misc.now(step), 1)
                elif kind == "p":
                    mixer, m = a
                    r = keys("sm").index(("sm", a)) % 2
                    n = 4 if mixer == "B" else 2
                    e = e_of(("sm", a))[0][0]
                    dve.wait_ge(read_act.sem, read_act.at(l, ("sm", a)))
                    settled(dve.tensor_scalar(coef[r][:, 0:n], sums[r][:, 0:n], 1e-30, None, ALU.max))
                    settled(dve.reciprocal(coef[r][:, 0:n], coef[r][:, 0:n]))
                    if mixer == "B":
                        c2 = coef[r].rearrange("p (t m) -> p m t", m=2)[:, 1, :]
                        settled(dve.tensor_scalar(c2, c2, nlam, None, ALU.mult))
                        for t, cols in enumerate((slice(0, P), slice(P, 384))):
                            ins = dve.tensor_scalar(eb[:, e + 1, cols], eb[:, e + 1, cols],
                                                    coef[r][:, 2 * t + 1:2 * t + 2], None, ALU.mult)
                        settled(ins)
                        for t, cols in enumerate((slice(0, P), slice(P, 384))):
                            ins = dve.scalar_tensor_tensor(out=eb[:, e, cols], in0=eb[:, e, cols],
                                                           scalar=coef[r][:, 2 * t:2 * t + 1], in1=eb[:, e + 1, cols],
                                                           op0=ALU.mult, op1=ALU.add)
                    else:
                        if mixer == "D":
                            gv = ng.rearrange("p (t j h) -> p j h t", t=NT, j=3)[:, 1 + m % 2, m // 2, :]
                            settled(dve.tensor_tensor(coef[r][:, 0:2], coef[r][:, 0:2], gv, ALU.mult))
                        for t, cols in enumerate((slice(0, P), slice(P, 384))):
                            ins = dve.tensor_scalar(eb[:, e, cols], eb[:, e, cols], coef[r][:, t:t + 1], None, ALU.mult)
                    ins.then_inc(dve_misc.now(step), 1)
                elif kind == "ngate":
                    dve.wait_ge(act_misc.sem, act_misc.at(l, step))
                    settled(dve.tensor_scalar(ng, ng, 1.0, None, ALU.add))
                    dve.reciprocal(ng, ng).then_inc(dve_misc.now(step), 1)
                elif kind == "cbuild":
                    dve.wait_ge(read_act.sem, read_act.at(l, ("qk", "Dc")))
                    kv = kcvt[:, :].rearrange("p (n j) -> p j n", j=CMP_STRIDE)
                    for half_ in range(2):
                        js = slice(half_ * 16, half_ * 16 + 16)
                        ins = dve.tensor_tensor(cblk[:, js, 0:NCMP], kv[:, :, half_:half_ + NCMP],
                                                pet[:, js].unsqueeze(2).to_broadcast([P, 16, NCMP]), ALU.add)
                    ins.then_inc(dve_misc.now(step), 1)
                elif kind == "cv":
                    dve.wait_ge(att_done.sem, att_done.at(l, step))
                    dve.tensor_copy(vcs[:, :], att[0:16, S1, 0:HD]).then_inc(read_dve.now(step), 1)
                elif kind == "cr":
                    dve.wait_ge(att_done.sem, att_done.at(l, step))
                    for h in range(H):
                        r = slice(32 * h, 32 * h + 32)
                        ins = dve.tensor_copy(vblk[r, h, :], att[r, TP, 0:HD])
                    ins.then_inc(read_dve.now(step), 1)
                elif kind == "cs":
                    dve.wait_ge(att_done.sem, att_done.at(l, step))
                    hv = csc[:, :, :, :].rearrange("p t (a b) n -> p b t a n", b=2)
                    for b in range(2):
                        for t in range(NT):
                            ins = dve.tensor_tensor(
                                hv[:, b, t, :, :], att[:, S0 + b, 32 * t:32 * t + 32].rearrange("p (a n) -> p a n", a=2),
                                cmask[:, t, :].unsqueeze(1).to_broadcast([P, 2, 16]), ALU.add)
                    ins.then_inc(read_dve.now(step), 1)
                    dve.wait_ge(read_dve.sem, read_dve.at(l, step))
                    flat = csc[:, :, :, :].rearrange("p t h n -> p (t h) n")
                    settled(dve.tensor_reduce(cmx, flat, AX.X, ALU.max))
                    dve.tensor_tensor(flat, flat, cmx.unsqueeze(2).to_broadcast([P, 8, 16]), ALU.subtract
                                      ).then_inc(cs_exp.now(step), 1)
                elif kind == "cp":
                    dve.wait_ge(act_misc.sem, act_misc.at(l, ("cs", None)))
                    flat = csc[:, :, :, :].rearrange("p t h n -> p (t h) n")
                    settled(dve.tensor_tensor(csc[:, :, :, :], csc[:, :, :, :],
                                              czero.unsqueeze(2).to_broadcast([P, NT, H, 16]), ALU.mult))
                    settled(dve.tensor_reduce(csum, flat, AX.X, ALU.add))
                    settled(dve.tensor_scalar(csum, csum, 1e-30, None, ALU.max))
                    settled(dve.reciprocal(csum, csum))
                    g0 = ng.rearrange("p (t j h) -> p t j h", t=NT, j=3)[:, :, 0, :]
                    c8 = csum.rearrange("p (t h) -> p t h", t=NT)
                    settled(dve.tensor_tensor(c8, c8, g0, ALU.mult))
                    dve.tensor_tensor(cpb[:, :, :, 0:16], csc[:, :, :, :],
                                      c8.unsqueeze(3).to_broadcast([P, NT, H, 16]), ALU.mult
                                      ).then_inc(dve_misc.now(step), 1)

            for l in range(DEPTH):
                for u in range(NCH + 1):
                    todo = steps_at(l, u)
                    for n, (ll, step) in enumerate(todo):
                        if rank(step) < 3:
                            do(ll, step)
                        if l == u == 0 and n < LEAD:
                            split(n)
                    if u == NCH:
                        continue
                    split(chunk(l, u) + LEAD)
                    for ll, step in todo:
                        if rank(step) == 3:
                            do(ll, step)

        @block.gpsimd
        def _(pool):
            chain = [0]

            def settled(ins):
                ins.then_inc(s_pool, 1)
                chain[0] += 1
                pool.wait_ge(s_pool, chain[0])

            def rsqrt(dst, sumsq, n, exps_):
                settled(pool.tensor_scalar(dst, sumsq, 1.0 / n, EPS, ALU.mult, ALU.add))
                return pool.tensor_tensor(dst, dst, exps_, ALU.pow)

            def rotate(v, table, r, shape, buf):
                h = r // 2
                a, b = buf
                cos, sin = table
                pool.tensor_tensor(a, v[..., 0:r], cos, ALU.mult)
                pool.tensor_tensor(b[..., 0:h], v[..., h:r], sin[..., 0:h], ALU.mult)
                settled(pool.tensor_tensor(b[..., h:r], v[..., 0:h], sin[..., h:r], ALU.mult))
                return pool.tensor_tensor(v[..., 0:r], a, b, ALU.add)

            def prep(v, rr, gains_, d, rope_):
                u = v.shape[2]
                settled(pool.tensor_tensor(v, v, rr.unsqueeze(3).to_broadcast([P, NT, u, d]), ALU.mult))
                n = u // len(gains_)
                for i, g in enumerate(gains_):
                    for t in range(NT):
                        ins = pool.tensor_tensor(v[:, t, i * n:(i + 1) * n, :], v[:, t, i * n:(i + 1) * n, :],
                                                 gn[:, g:g + d].unsqueeze(1).to_broadcast([P, n, d]), ALU.mult)
                settled(ins)
                r = d // 4
                for t in range(NT):
                    a = rot1[:, t * P:t * P + u * r].rearrange("p (u r) -> p u r", r=r)
                    b = rot2[:, t * P:t * P + u * r].rearrange("p (u r) -> p u r", r=r)
                    cos = rope_[:, t, 0, :].unsqueeze(1).to_broadcast([P, u, r])
                    sin = rope_[:, t, 1, :].unsqueeze(1).to_broadcast([P, u, r])
                    ins = rotate(v[:, t, :, :], (cos, sin), r, None, (a, b))
                return ins

            pool.memset(half, -0.5).then_inc(s_phalf, 1)
            pool.wait_ge(s_phalf, 1)
            pool.wait_ge(s_const, 16)
            for l in range(DEPTH):
                for u in range(NCH):
                    for step in STEPS[u]:
                        kind, a = step
                        if kind == "stats":
                            pool.wait_ge(act_misc.sem, act_misc.at(l, step))
                            rsqrt(xr[a], xss, D_MODEL, half[:, 0:NT]).then_inc(pool_done.now(step), 1)
                        elif kind == "prep":
                            pool.wait_ge(dve_misc.sem, dve_misc.at(l, step))
                            pool.wait_ge(s_small, 48 * (l + 1))
                            d = DD if a == "B" else HD
                            n = NT * 2 * MIX // d
                            settled(rsqrt(rs[:, 0:n], ss[:, 0:n], d, half[:, 0:n]))
                            rr = rs[:, 0:n].rearrange("p (t u) -> p t u", t=NT)
                            if a == "D":
                                v = proj[:, :, NSQ:NSQ + MIX].rearrange("p t (u d) -> p t u d", d=HD)
                                settled(prep(v, rr[:, :, 0:H], (G_NQ,), HD, rope64))
                                ins = prep(kdup[:, :, :, :], rr[:, :, H:2 * H], (G_KS, G_KW), HD, rope64)
                            else:
                                c0 = DFQ if a == "B" else MBQ
                                v = proj[:, :, c0:c0 + 2 * MIX].rearrange("p t (u d) -> p t u d", d=d)
                                ins = prep(v, rr, (G_DQ, G_DK) if a == "B" else (G_MQ, G_MK), d,
                                           rope32 if a == "B" else rope64)
                            ins.then_inc(pool_done.now(step), 1)
                            pool.wait_ge(pool_done.sem, pool_done.at(l, step))
                        elif kind == "kcprep":
                            pool.wait_ge(dve_misc.sem, dve_misc.at(l, step))
                            settled(rsqrt(kcr, kcss, HD, half[0:16, 0:2]))
                            v = kcs[:, :, :]
                            settled(pool.tensor_tensor(v, v, kcr.unsqueeze(2).to_broadcast([16, 2, HD]), ALU.mult))
                            settled(pool.tensor_tensor(v, v, gn[0:16, G_KC:G_KC + HD].unsqueeze(1).to_broadcast([16, 2, HD]), ALU.mult))
                            r = HD // 4
                            bufs = [b[0:16, 0:2 * r].rearrange("p (u r) -> p u r", r=r) for b in (rot1, rot2)]
                            cs_ = [ropec[:, i, :].unsqueeze(1).to_broadcast([16, 2, r]) for i in range(2)]
                            rotate(v, cs_, r, None, bufs).then_inc(pool_done.now(step), 1)
                            pool.wait_ge(pool_done.sem, pool_done.at(l, step))
                        elif kind == "subln":
                            pool.wait_ge(read_act.sem, read_act.at(l, ("o", "B")))
                            if l:
                                pool.wait_ge(dve_misc.sem, dve_misc.at(l - 1, step))
                            ob = osb[:, :, MIX:2 * MIX]
                            pool.tensor_tensor(osq[:, :, :], ob, ob, ALU.mult).then_inc(sub_sq.now(step), 1)
                            pool.wait_ge(dve_misc.sem, dve_misc.at(l, step))
                            settled(rsqrt(obr, obss, HD, half[:, 0:8]))
                            settled(pool.tensor_scalar(obr, obr, 1.0 - lam_init(l), None, ALU.mult))
                            obv = ob.rearrange("p t (h d) -> p t h d", d=HD)
                            settled(pool.tensor_tensor(obv, obv, obr.rearrange("p (t h) -> p t h", t=NT).unsqueeze(3)
                                                       .to_broadcast([P, NT, H, HD]), ALU.mult))
                            for t in range(NT):
                                ins = pool.tensor_tensor(obv[:, t, :, :], obv[:, t, :, :], gn[:, G_SUB:G_SUB + HD].unsqueeze(1)
                                                         .to_broadcast([P, H, HD]), ALU.mult)
                            ins.then_inc(pool_done.now(step), 1)
                            pool.wait_ge(pool_done.sem, pool_done.at(l, step))
                        elif kind == "merge" and a[0] in (1, 2):
                            pool.wait_ge(dve_acc.sem, dve_acc.at(l, step))
                            cols = slice(a[1] * NC, (a[1] + 1) * NC)
                            pool.tensor_tensor(merged[:, :, cols], merged[:, :, cols], prod[:, :, cols], ALU.add
                                               ).then_inc(pool_done.now(step), 1)


def lam_init(l):
    return 0.8 - 0.6 * math.exp(-0.3 * l)


def rope_table(positions, width):
    r = width // 4
    inv = np.float32(500000.0) ** (-np.arange(r // 2, dtype=np.float32) * np.float32(2.0) / np.float32(r))
    ang = positions.astype(np.float32)[:, None] * inv[None, :].astype(np.float32)
    c, s = np.cos(ang).astype(np.float32), np.sin(ang).astype(np.float32)
    return np.concatenate([c, c, -s, s], axis=1)


def constants():
    p = np.arange(P)
    c = np.zeros((P, C_END), np.float32)
    c[:, C_ID:C_ID + P] = np.eye(P)
    c[:, C_TRI:C_TRI + P] = -(p[:, None] >= p[None, :]).astype(np.float32)
    c[:, C_ONE:C_ONE + P] = -1.0
    pos = np.arange(SEQ)
    tile = lambda t: t.reshape(NT, P, -1).transpose(1, 0, 2).reshape(P, -1)
    c[:, C_R32:C_R32 + 32] = tile(rope_table(pos, DD))
    c[:, C_R64:C_R64 + 64] = tile(rope_table(pos, HD))
    ends = CMP_STRIDE * np.arange(16) + CMP_LEN - 1
    seen = (ends[None, :] <= pos[:, None]) & (np.arange(16)[None, :] < NCMP)
    c[:, C_CM:C_CM + 32] = tile(np.where(seen, 0.0, NEG).astype(np.float32))
    c[:, C_CZ:C_CZ + 32] = tile(seen.astype(np.float32))
    c[0:16, C_RC:C_RC + 32] = rope_table(ends, HD)
    for h in range(H):
        c[0:16, C_REP + 32 * h:C_REP + 32 * h + 16] = np.eye(16)
    m = np.zeros((P, P + 2 * 384), np.float32)
    m[:, 0:P] = np.eye(P)
    strict = np.where(p[:, None] < p[None, :], 0.0, NEG)
    causal = np.where(p[None, :] <= p[:, None], 0.0, NEG)
    for at, mask in ((P, strict), (P + 384, causal)):
        m[:, at:at + P] = mask
        m[:, at + 256:at + 384] = mask
    return c, m


def kernel(x, attn_norm_g, w_in, diff_qn_g, diff_kn_g, diff_lam, diff_subln_g, moba_qn_g, moba_kn_g,
           nsa_qn_g, nsa_kn_g, nsa_cmp_pe, nsa_cmp_w, w_gate, b_gate, w_branch, w_out, ffn_norm_g,
           w_ffn_gate, w_ffn_up, w_ffn_down):
    import concourse.bacc as bacc
    from concourse.bass_utils import run_bass_kernel_spmd as run

    L = DEPTH
    arr = lambda a: np.ascontiguousarray(a)
    columns = lambda g: np.asarray(g).reshape(L, KT, P).transpose(0, 2, 1)
    const, masks = constants()
    arrays = {
        "x": x, "w_in": w_in, "w_gate": w_gate, "w_branch": w_branch, "w_out": w_out,
        "w_ffn_gate": w_ffn_gate, "w_ffn_up": w_ffn_up, "w_ffn_down": w_ffn_down,
        "norm_g": np.concatenate([columns(attn_norm_g), columns(ffn_norm_g)], axis=2),
        "gains": np.concatenate([np.asarray(a).reshape(L, -1) for a in (
            diff_qn_g, diff_kn_g, moba_qn_g, moba_kn_g, nsa_qn_g, nsa_kn_g, diff_subln_g)], axis=1),
        "lam": np.asarray(diff_lam),
        "cmp_pe": np.asarray(nsa_cmp_pe).transpose(0, 1, 3, 2).reshape(L, P, CMP_LEN),
        "cmp_w": np.asarray(nsa_cmp_w).reshape(L, 2, CMP_LEN, HD, HD).transpose(0, 1, 3, 2, 4)
                   .reshape(L, P, CMP_LEN, HD),
        "b_gate": b_gate, "const": const, "masks": masks,
    }
    nc = bacc.Bacc("TRN2", target_bir_lowering=False, num_devices=1)
    feeds, args = {}, {}
    for name, a in arrays.items():
        a = arr(a)
        feeds[f"in_{name}"] = a
        args[name] = nc.dram_tensor(f"in_{name}", a.shape, mybir.dt.from_np(a.dtype), kind="ExternalInput").ap()
    out = nc.dram_tensor("out_x", (1, SEQ, D_MODEL), F32, kind="ExternalOutput").ap()
    trunk_kernel(nc, **args, out=out)
    r = run(nc, [feeds], core_ids=[0])
    return r.results[0]["out_x"]
```

```python
import math
from contextlib import ExitStack

import numpy as np

from concourse import mybir

ALU = mybir.AluOpType
ACT = mybir.ActivationFunctionType
AX = mybir.AxisListType
F32 = mybir.dt.float32
F32R = mybir.dt.float32r
BF16 = mybir.dt.bfloat16

P = 128
SEQ, D_MODEL, DEPTH = 256, 1024, 2
NT = SEQ // P
KT = D_MODEL // P
H, HD = 4, 64
MIX = H * HD
DD = HD // 2
IN_COLS = 10 * MIX + 6 * HD + 3 * H
FFN = 2816
FC = 256
NC = 512
CMP_LEN, CMP_STRIDE, NCMP = 32, 16, 15
EPS = 1e-6
NEG = -1e30

SBQ, SBV, DFQ, DFK, DFV, MBQ, MBK, MBV, NSQ = (MIX * i for i in (0, 2, 3, 4, 5, 6, 7, 8, 9))
NKC = 10 * MIX
NKS, NVS, NKW, NVW, NGT = (NKC + HD * i for i in (2, 3, 4, 5, 6))

G_DQ, G_DK, G_MQ, G_MK, G_NQ, G_KC, G_KS, G_KW, G_SUB = 0, 32, 64, 128, 192, 256, 320, 384, 448

C_ID, C_TRI, C_ONE, C_R32, C_R64, C_CM, C_CZ, C_RC, C_REP, C_END = 0, 128, 256, 384, 416, 480, 512, 544, 576, 704

N_IN, N_GATE, N_FFN, N_DOWN = -(-IN_COLS // NC), 8, FFN // FC, FFN // P // 2
CHUNKS = ([("in", g, q) for g in range(N_IN) for q in range(4)]
          + [("gate", g, q) for g in range(N_GATE) for q in range(4)]
          + [("branch", i, c) for c in range(2) for i in range(4)]
          + [("out", q, c) for q, c in ((0, 0), (1, 0), (0, 1), (2, 0), (3, 0), (1, 1), (2, 1), (3, 1))]
          + [("ffn", j, q) for j in range(N_FFN) for q in range(4)]
          + [("down", j, c) for c in range(2) for j in range(N_DOWN)])
NCH = len(CHUNKS)
U_GATE, U_BR, U_OUT, U_FFN, U_DOWN = (next(n for n, c in enumerate(CHUNKS) if c[0] == k)
                                      for k in ("gate", "branch", "out", "ffn", "down"))
RESULTS = ([("proj", g) for g in range(N_IN)] + [("zg", g) for g in range(N_GATE)]
           + [("merge", (i, c)) for c in range(2) for i in range(4)] + [("xadd", ("out", c)) for c in range(2)]
           + [("act", j) for j in range(N_FFN)] + [("xadd", ("down", c)) for c in range(2)])


def bank_pair(l, step):
    return 2 * ((l * len(RESULTS) + RESULTS.index(step)) % 2)


EARLY = (-4, -3)
WARM_UP = 6, 3
RAW, WR, LEAD = 4, 4, 2


def in_cols(g):
    return min(NC, IN_COLS - g * NC)


PLAN = {
    "stats": 1, "lambda": 16, "x": (0, 0, 1, 1), "f": (-2, -1, 1, 2), "m": (-2, -1, 2, 3), "h": 5, "sig": (52, 53, 55, 57),
    "o": (22, 42, 52, 54), "subln": 33, "prep": (13, 19, 26), "ngate": 26,
    "Aq": 5, "Ak": 6, "Az": (7, 9, 11, 14), "Asp": (9, 10, 12, 18),
    "Acum": (10, 11, 17, 20), "Apv": (11, 17, 18, 21), "Ao": 21,
    "Bq": 19, "Bk": 20, "Bsm": (22, 24, 27, 28), "Bp": (22, 24, 27, 29),
    "Bpt": (24, 27, 29, 31), "Bpv": (27, 28, 31, 32), "Bo": 32,
    "Cq": 30, "Ck": 32, "Csm": (34, 34, 37, 37), "Cp": (35, 36, 38, 38),
    "Cpt": (37, 38, 39, 40), "Cpv": (39, 39, 40, 41), "Co": 42,
    "Dc": 28, "cbuild": 29, "ck": 30, "cv": 33, "kcprep": 32, "kct": 34, "cr": 34, "cs": 38, "cp": 39, "cpt": 41, "cpv": 43,
    "Dq": 33, "Dk": 36, "Dsm": (40, 40, 42, 43, 44, 45, 46, 47),
    "Dp": (41, 42, 43, 44, 45, 46, 47, 48),
    "Dpt": (43, 44, 45, 46, 47, 48, 50, 51),
    "Dpv": (45, 45, 46, 47, 48, 50, 51, 52), "Do": 53,
}
RANK = {
    "x0": 0, "f0": 0, "m0": 0,
    "proj": 1, "zg": 1, "merge": 1, "xadd": 1, "act": 1,
    "Acum": 1.5, "Dp": 1.5, "cpv": 1.5, "sig": 1.5,
    "Cpv": 2, "cbuild": 2, "kct": 2,
    "x": 2.5, "Asp": 2.5, "Bpv": 2.5, "ck": 2.5,
    "cv": 3, "cs": 3,
    "prep": 3.5, "Csm": 3.5, "Dpv": 3.5, "lambda": 3.5, "stats": 3.5,
    "subln": 4.5, "Bsm": 4.5, "Bpt": 4.5,
    "ngate": 5, "Cp": 5, "h": 5,
    "kcprep": 5.5,
    "f": 6, "Bp": 6,
}


def steps():
    at = {u: [] for u in range(NCH + 2)}

    def put(u, *step):
        at[u].append(step)

    for kp in range(KT // 2):
        put(PLAN["x"][kp], "pair", ("x", kp))
        put(U_FFN + PLAN["f"][kp], "pair", ("f", kp))
        put(U_OUT + PLAN["m"][kp], "pair", ("m", kp))
        put(PLAN["o"][kp], "pair", ("o", kp))
    put(PLAN["stats"], "stats", "x")
    put(U_FFN + PLAN["stats"], "stats", "f")
    for g in range(N_IN):
        put(4 * g + 4, "proj", g)
    for name in ("Aq", "Ak", "Bq", "Bk", "Cq", "Ck", "Dc", "Dq", "Dk"):
        put(PLAN[name], "qk", name)
    for mixer in "ABCD":
        if mixer != "A":
            put(PLAN["prep"]["BCD".index(mixer)], "prep", mixer)
        for h in range(2 * H if mixer == "D" else H):
            for kind in ("z", "sp", "cum", "pv") if mixer == "A" else ("sm", "p", "pt", "pv"):
                put(PLAN[mixer + kind][h], kind, h if mixer == "A" and kind != "pv" else (mixer, h))
        put(PLAN[mixer + "o"], "o", mixer)
    for kind in ("lambda", "subln", "ngate", "cbuild", "ck", "cv", "kcprep", "kct", "cr", "cs", "cp", "cpt", "cpv"):
        put(PLAN[kind], kind, None)
    for g in range(N_GATE):
        put(U_GATE + 4 * g + 4, "zg", g)
    for i in range(4):
        put(PLAN["sig"][i], "sig", i)
        for c in range(2):
            put(U_BR + 4 * c + i + 1, "merge", (i, c))
    for c in range(2):
        put(CHUNKS.index(("out", 3, c)) + 1, "xadd", ("out", c))
        put(U_DOWN + N_DOWN * (c + 1), "xadd", ("down", c))
    for j in range(N_FFN):
        put(U_FFN + 4 * j + 4, "act", j)
        put(U_FFN + 4 * j + PLAN["h"], "pair", ("h", j))
    return {u: sorted(s, key=rank) for u, s in at.items()}


def name_of(step):
    kind, a = step
    if kind == "pair":
        return a[0] if a[0] in "oh" or a[1] else a[0] + "0"
    if kind in ("sm", "p", "pt", "pv"):
        return a[0] + kind
    if kind in ("z", "sp", "cum"):
        return "A" + kind
    return kind


def rank(step):
    return RANK.get(name_of(step), 4)


STEPS = steps()


def steps_at(l, u):
    early = [("pair", ("x", kp)) for kp in range(2)]
    if u == NCH:
        return [(l, s) for s in STEPS[u]] if l == DEPTH - 1 else []
    todo = [(l, s) for s in STEPS[u] if not (l and s in early)]
    if l and u == 0:
        todo = [(l - 1, s) for s in STEPS[NCH]] + todo
    if l < DEPTH - 1:
        todo += [(l + 1, s) for kp, s in enumerate(early) if u == NCH + EARLY[kp]]
    return todo


ORDER = [s for u in range(NCH + 1) for s in STEPS[u]]


def keys(*kinds):
    return [s for s in ORDER if s[0] in kinds]


class Events:

    def __init__(self, sem, order):
        self.sem, self.order, self.count = sem, order, 0
        self.place = {k: n for n, k in enumerate(order)}

    def at(self, layer, key):
        return layer * len(self.order) + self.place[key] + 1

    def now(self, key):
        assert self.order[self.count % len(self.order)] == key, (key, self.order[self.count % len(self.order)])
        self.count += 1
        return self.sem


TP, OB, S0, S1 = range(4)


def banks_of(step):
    kind, a = step
    if kind == "pair":
        if a[0] == "o":
            return (TP,)
        return ((S0, S1)[a[1] % 2],) if a[0] == "h" else ((TP, S0, S1, OB)[a[1]],)
    if kind in ("qk", "pt", "kct", "cpt", "cr"):
        return (TP,)
    if kind in ("z", "cum"):
        return ((S0, S1)[a % 2],)
    if kind == "sm":
        return (S0, S1) if a[0] == "B" else ((S0, S1)[a[1] % 2],)
    if kind == "cs":
        return (S0, S1)
    if kind == "ck":
        return (S0,)
    if kind == "cv":
        return (S1,)
    if kind == "o":
        return (OB,)
    return ()


def reader_of(step):
    kind, a = step
    by_dve = kind in ("pair", "cs", "cv", "cr", "kct") or (kind == "qk" and a != "Dc") or (kind == "o" and a in "BC")
    return "dve" if by_dve else "act"


BANK_STEPS = [s for s in ORDER if banks_of(s)]
BANK_USES = {b: [s for s in BANK_STEPS if b in banks_of(s) and s[0] != "cum"] for b in range(4)}


def e_of(step):
    kind, a = step
    if kind == "z":
        return (2 * (a % 2), 2 * (a % 2) + 1), ("cum", a)
    if kind == "sm" and a[0] == "B":
        return (2 * (a[1] % 2), 2 * (a[1] % 2) + 1), ("pt", a)
    return (a[1] % 4,), ("pt", a)


E_STEPS = [s for s in ORDER if s[0] in ("z", "sm")]
PT_STEPS = [s for s in ORDER if s[0] in ("cum", "pt")]


def pv_step(s):
    return ("pv", ("A", s[1])) if s[0] == "cum" else ("pv", s[1])


def trunk_kernel(nc, x, w_in, w_gate, w_branch, w_out, w_ffn_gate, w_ffn_up, w_ffn_down,
                 norm_g, gains, lam, cmp_pe, cmp_w, b_gate, const, masks, out):
    with ExitStack() as ctx:
        def sem(name):
            return ctx.enter_context(nc.semaphore(name))

        base = nc.sbuf_base + (-nc.sbuf_base) % 64
        top = [base]

        def place(name, shape, dt, at=None):
            size = int(np.prod(shape[1:])) * (2 if dt == BF16 else 4)
            offset = top[0] if at is None else at
            if at is None:
                top[0] += size + (-size) % 32
            return nc.alloc_sbuf_tensor_at(name, shape, dt, offset=offset)

        w_raw = place("w_raw", [P, RAW, 2, NC], F32)
        w_hi = place("w_hi", [P, WR, 2, NC], F32R)
        w_lo = place("w_lo", [P, WR, 2, NC], F32R)
        xs = place("xs", [P, NT, D_MODEL], F32)
        xt_hi = place("xt_hi", [P, KT, SEQ], F32R)
        xt_lo = place("xt_lo", [P, KT, SEQ], F32R)
        ot_hi = place("ot_hi", [P, KT, SEQ], F32R)
        ot_lo = place("ot_lo", [P, KT, SEQ], F32R)
        big = top[0]
        proj = place("proj", [P, NT, IN_COLS], F32)
        zg = place("zg", [P, NT, 4, D_MODEL], F32)
        zg_at = big + NT * IN_COLS * 4
        zg_at += (-zg_at) % 32
        end_big = top[0]
        squares = place("squares", [P, NT, NC], F32, at=zg_at)
        merged = place("merged", [P, NT, D_MODEL], F32, at=big)
        prod = place("prod", [P, NT, D_MODEL], F32, at=big + 4 * NT * D_MODEL)
        ht_hi = place("ht_hi", [P, FFN // P, SEQ], F32R, at=big)
        ht_lo = place("ht_lo", [P, FFN // P, SEQ], F32R, at=big + 4 * FFN // P * SEQ)
        assert big + 8 * FFN // P * SEQ <= end_big
        osb = place("osb", [P, NT, D_MODEL], F32)
        kcdup = osb[:, :, 3 * MIX:].rearrange("p t (m a d) -> p t m a d", m=2, a=2)
        bg = place("bg", [P, 2, D_MODEL], F32)
        big2 = top[0]
        cw = place("cw", [P, 2, CMP_STRIDE, HD], F32)
        silu = place("silu", [P, NT, FC], F32, at=big2)
        hid = place("hid", [P, 2, NT, FC], F32, at=big2 + 4 * NT * FC)
        qk_hi = [place(f"qk_hi{i}", [P, 4, SEQ], F32R) for i in range(2)]
        qk_lo = [place(f"qk_lo{i}", [P, 4, SEQ], F32R, at=zg_at + 4 * D_MODEL * (4 * i + 3)) for i in range(2)]
        kc_hl = place("kc_hl", [P, 2, 16], F32R)
        kcvt = place("kcvt", [P, 2, SEQ], F32)
        sp_at = top[0]
        eb = place("eb", [P, 4, 384], F32)
        sp_parts = [place(f"sp_parts{i}", [P, 2, 384], F32R, at=sp_at + 4 * 2 * 384 * i) for i in range(2)]
        ptb = place("ptb", [P, 2, 384], F32)
        ptc = place("ptc", [P, NT, P], F32)
        warm = place("warm", [P, NC], BF16, at=top[0] - 4 * NT * P)
        cblk = place("cblk", [P, 2, CMP_STRIDE, 16], F32)
        vblk = place("vblk", [P, H, HD], F32)
        cst = place("cst", [P, C_END], F32)
        tri_r = place("tri_r", [P, 2, P], F32R)
        cst16 = place("cst16", [P, 3 * P], BF16)
        gn = place("gn", [P, 512], F32)
        gt = place("gt", [P, 2 * KT], F32)
        pet = place("pet", [P, 2, CMP_STRIDE], F32)
        lamb = place("lamb", [P, 4, DD], F32)
        rot_at = top[0]
        rot1 = place("rot1", [P, 256], F32)
        rot2 = place("rot2", [P, 256], F32)
        kdup = place("kdup", [P, NT, 4, HD], F32)
        kcs = place("kcs", [16, 2, HD], F32)
        csc = place("csc", [P, NT, H, 16], F32)
        cpb = place("cpb", [P, NT, H, 32], F32)
        vcs = place("vcs", [16, HD], F32)
        osq = place("osq", [P, NT, MIX], F32, at=rot_at)
        rot_l = place("rot_l", [P, 2 * DD], F32)
        small = place("small", [P, 256], F32)
        kcsq = place("kcsq", [16, 2, HD], F32)
        assert top[0] <= nc.sbuf_usable_end, top[0] - nc.sbuf_usable_end

        sm = lambda a, n: small[:, a:a + n]
        xss, xr = sm(0, 2), {"x": sm(2, 2), "f": sm(4, 2)}
        half = sm(8, 32)
        ss, rs = sm(40, 32), sm(72, 32)
        stat = [sm(104 + 4 * i, 4) for i in range(2)]
        nbias = [sm(112 + 4 * i, 4) for i in range(2)]
        sums = [sm(120 + 4 * i, 4) for i in range(2)]
        coef = [sm(128 + 4 * i, 4) for i in range(2)]
        row = {m: sm(216 + 8 * i, 8).rearrange("p (t h) -> p t h", t=NT) for i, m in enumerate("BC")}
        ng = sm(136, 24)
        cmx, csum = sm(160, 8), sm(168, 8)
        nlam, lsum, lexp = sm(176, 1), sm(178, 2), sm(180, 2)
        kcss, kcr = small[0:16, 184:186], small[0:16, 186:188]
        obss = sm(190, 8)
        obr = sm(200, 8)

        acc = [ctx.enter_context(nc.psum_tensor(f"acc{i}", [P, NC], F32)) for i in range(4)]
        att = ctx.enter_context(nc.psum_tensor("att", [P, 4, NC], F32))

        masks32 = eb[:, 0, 0:2 * P]
        ident, negtri, negone = cst[:, C_ID:C_ID + P], cst[:, C_TRI:C_TRI + P], cst[:, C_ONE:C_ONE + P]
        ident16, mask_a, mask_s = (cst16[:, i * P:(i + 1) * P] for i in range(3))
        rope32 = cst[:, C_R32:C_R32 + 32].rearrange("p (t a r) -> p t a r", t=NT, a=2)
        rope64 = cst[:, C_R64:C_R64 + 64].rearrange("p (t a r) -> p t a r", t=NT, a=2)
        cmask = cst[:, C_CM:C_CM + 32].rearrange("p (t n) -> p t n", t=NT)
        czero = cst[:, C_CZ:C_CZ + 32].rearrange("p (t n) -> p t n", t=NT)
        ropec = cst[0:16, C_RC:C_RC + 32].rearrange("p (a r) -> p a r", a=2)

        s_ident = sem("identity_landed")
        s_const = sem("const_landed")
        s_mask = sem("masks_landed")
        s_mask16 = sem("masks_in_bf16")
        s_gt = sem("norm_gains_landed")
        s_x = [sem(f"x_quarter_landed{kp}") for kp in range(KT // 2)]
        s_raw = [sem(f"raw_landed{i}") for i in range(RAW)]
        s_small = sem("layer_params_landed")
        s_cw = sem("cmp_w_landed")
        s_bg = [sem(f"bias_landed{i}") for i in range(2)]
        s_out = sem("out_written")
        s_tile = sem("last_chunk_tile_done")
        s_tsum = sem("last_tile_added")
        s_hi = sem("w_hi_ready")
        s_lo = sem("w_lo_ready")
        s_ch = sem("chunk_done")
        s_init = sem("buffers_cleared")
        s_warm = sem("zeros_ready")

        att_keys = [s for s in ORDER if (banks_of(s) and s[0] != "o") or s[0] in ("pv", "cpv")]
        att_done = Events(sem("att_done"), att_keys)
        read_act = Events(sem("att_read_act"), [s for s in BANK_STEPS if reader_of(s) == "act" and s[0] != "z"])
        read_dve = Events(sem("att_read_dve"), [s for s in BANK_STEPS if reader_of(s) == "dve"])
        hi_done = Events(sem("hi_done"), [s for s in keys("pair", "qk", "kct") if s[1] != "Dc"])
        proj_out = Events(sem("proj_read"), keys("proj"))
        act_misc = Events(sem("scalar_small"), [s for s in ORDER if s[0] in (
            "stats", "lambda", "prep", "ngate", "kcprep", "cs", "sig", "act")])
        dve_acc = Events(sem("acc_read_dve"), keys("zg", "merge", "xadd", "act"))
        dve_misc = Events(sem("vector_small"), [s for s in ORDER if s[0] in (
            "lambda", "prep", "ngate", "kcprep", "subln", "cbuild", "sm", "p", "sp", "cp")])
        merged_done = Events(sem("merged_done"), [s for s in keys("merge") if s[1][0] == 3])
        cs_max = Events(sem("cs_max_done"), keys("cs"))
        lam_sums = Events(sem("lambda_sums"), keys("lambda"))
        s_zc = sem("softplus_chain")
        s_kd = sem("kdup_ready")
        s_dve = sem("vector_chain")
        s_pool = sem("gpsimd_chain")
        s_phalf = sem("exponent_set")
        sub_sq = Events(sem("subln_squares"), keys("subln"))
        pool_done = Events(sem("gpsimd_done"), [s for s in ORDER if s[0] in (
            "stats", "prep", "kcprep", "subln") or (s[0] == "merge" and s[1][0] in (1, 2))])

        def chunk(l, u):
            return l * NCH + u

        def weight(l, u):
            kind, a, b = CHUNKS[u]
            if kind == "in":
                n = in_cols(a)
                return [(w_in[l, 2 * b * P:(2 * b + 2) * P, a * NC:a * NC + n], slice(0, n))]
            if kind == "gate":
                return [(w_gate[l, a // 2, 2 * b * P:(2 * b + 2) * P, (a % 2) * NC:(a % 2 + 1) * NC], slice(0, NC))]
            if kind == "branch":
                return [(w_branch[l, a, :, b * NC:(b + 1) * NC], slice(0, NC))]
            if kind == "out":
                return [(w_out[l, 2 * a * P:(2 * a + 2) * P, b * NC:(b + 1) * NC], slice(0, NC))]
            if kind == "ffn":
                rows = slice(2 * b * P, (2 * b + 2) * P)
                return [(w_ffn_gate[l, rows, a * FC:(a + 1) * FC], slice(0, FC)),
                        (w_ffn_up[l, rows, a * FC:(a + 1) * FC], slice(FC, 2 * FC))]
            return [(w_ffn_down[l, 2 * a * P:(2 * a + 2) * P, b * NC:(b + 1) * NC], slice(0, NC))]

        def raw_value(n):
            return 16 * sum(2 if CHUNKS[m % NCH][0] == "ffn" else 1 for m in range(n % RAW, n + 1, RAW))

        def width(u):
            return in_cols(CHUNKS[u][1]) if CHUNKS[u][0] == "in" else NC

        def previous(l, uses, step):
            n = uses.index(step)
            return (l, uses[n - 1]) if n else ((l - 1, uses[-1]) if l else None)

        block = ctx.enter_context(nc.Block())

        @block.sync
        def _(sp):
            def load_chunk(n):
                l, u = divmod(n, NCH)
                if n >= RAW:
                    sp.wait_ge(s_lo, n - RAW + 1)
                for src, cols in weight(l, u):
                    sp.dma_start(w_raw[:, n % RAW, :, cols], src.rearrange("(k p) n -> p k n", p=P)
                                 ).then_inc(s_raw[n % RAW], 16)

            def load_x(kp):
                cols = slice(2 * kp * P, (2 * kp + 2) * P)
                sp.dma_start(xs[:, :, cols], x[0, :, cols].rearrange("(t p) d -> p t d", p=P)).then_inc(s_x[kp], 16)

            load_x(0)
            sp.dma_start(ident, const[:, C_ID:C_ID + P]).then_inc(s_ident, 16)
            sp.dma_start(gt[:, :], norm_g[0]).then_inc(s_gt, 16)
            load_chunk(0)
            load_x(1)
            load_chunk(1)
            load_x(2)
            load_x(3)
            for l in range(DEPTH):
                for u in range(NCH):
                    if chunk(l, u) > 1:
                        load_chunk(chunk(l, u))
                    if u == 3 and l == 0:
                        sp.dma_start(cst[:, C_ID + P:], const[:, C_ID + P:]).then_inc(s_const, 16)
                        sp.dma_start(masks32, masks).then_inc(s_mask, 16)
                    if u == 8:
                        if l:
                            sp.wait_ge(pool_done.sem, pool_done.at(l - 1, ("stats", "f")))
                        sp.dma_start(gn[:, :], gains[l].partition_broadcast(P)).then_inc(s_small, 16)
                        sp.dma_start(lamb[:, :, :], lam[l].partition_broadcast(P)).then_inc(s_small, 16)
                        sp.dma_start(pet[:, :, :], cmp_pe[l]).then_inc(s_small, 16)
                    if u == 12:
                        if l:
                            sp.wait_ge(att_done.sem, att_done.at(l - 1, ("pair", ("h", N_FFN - 1))))
                        sp.dma_start(cw[:, :, :, :], cmp_w[l]).then_inc(s_cw, 16)
                    if CHUNKS[u][0] == "gate" and CHUNKS[u][1] % 2 == 0 and CHUNKS[u][2] == 0:
                        i = CHUNKS[u][1] // 2
                        if i >= 2:
                            sp.wait_ge(dve_acc.sem, dve_acc.at(l, ("zg", 2 * i - 3)))
                        elif l:
                            sp.wait_ge(dve_acc.sem, dve_acc.at(l - 1, ("zg", 2 * i + 5)))
                        sp.dma_start(bg[:, i % 2, :], b_gate[l, i].partition_broadcast(P)
                                     ).then_inc(s_bg[i % 2], 16)
                    if u == U_FFN + 6 and l + 1 < DEPTH:
                        sp.wait_ge(read_dve.sem, read_dve.at(l, ("pair", ("f", KT // 2 - 1))))
                        sp.dma_start(gt[:, :], norm_g[l + 1]).then_inc(s_gt, 16)
            y = out[0].rearrange("(t p) d -> p t d", p=P)
            sp.wait_ge(dve_acc.sem, dve_acc.at(DEPTH - 1, ("xadd", ("down", 0))))
            sp.dma_start(y[:, :, 0:NC], xs[:, :, 0:NC]).then_inc(s_out, 16)
            sp.wait_ge(s_tsum, 1)
            sp.dma_start(y[:, 0, NC:], xs[:, 0, NC:]).then_inc(s_out, 16)
            sp.wait_ge(dve_acc.sem, dve_acc.at(DEPTH - 1, ("xadd", ("down", 1))))
            sp.dma_start(y[:, 1, NC:], xs[:, 1, NC:]).then_inc(s_out, 16)
            sp.wait_ge(s_out, 48)

        @block.tensor
        def _(pe):
            def bank_free(l, step):
                for b in banks_of(step):
                    prev = previous(l, BANK_USES[b], step)
                    if prev:
                        before = ("cum", prev[1][1]) if prev[1][0] == "z" else prev[1]
                        ev = read_dve if reader_of(before) == "dve" else read_act
                        pe.wait_ge(ev.sem, ev.at(prev[0], before))

            def products(l, u):
                kind, a, b = CHUNKS[u]
                n = chunk(l, u)
                if n == 0:
                    pe.wait_ge(s_hi, 1)
                else:
                    pe.wait_ge(s_lo, n + 1)
                N = width(u)
                first, last = {"in": (b == 0, b == 3), "gate": (b == 0, b == 3), "branch": (True, True),
                               "out": (a == 0, a == 3), "ffn": (b == 0, b == 3),
                               "down": (a == 0, a == N_DOWN - 1)}[kind]
                hi, lo, k0 = {"branch": (ot_hi, ot_lo, 2 * a), "out": (xt_hi, xt_lo, 2 * a),
                              "down": (ht_hi, ht_lo, 2 * a)}.get(kind, (xt_hi, xt_lo, 2 * b))
                src = {"in": ("x", b) if a == 0 else None, "ffn": ("f", b) if a == 0 else None, "gate": None,
                       "branch": ("o", a) if b == 0 else None, "out": ("m", a) if b == 0 else None,
                       "down": ("h", a) if b == 0 else None}[kind]
                if src:
                    pe.wait_ge(hi_done.sem, hi_done.at(l, ("pair", src)))
                step = {"in": ("proj", a), "gate": ("zg", a), "branch": ("merge", (a, b)), "out": ("xadd", ("out", b)),
                        "ffn": ("act", a), "down": ("xadd", ("down", b))}[kind]
                pair = bank_pair(l, step)
                g = l * len(RESULTS) + RESULTS.index(step) - 2
                if first and g >= 0:
                    ll, before = g // len(RESULTS), RESULTS[g % len(RESULTS)]
                    ev = proj_out if before[0] == "proj" else dve_acc
                    pe.wait_ge(ev.sem, ev.at(ll, before))
                wh = w_hi[:, n % WR, :, :]
                wl = w_lo[:, n % WR, :, :]

                def product(x_part, w_part, t, k, first=False, last=False):
                    return pe.matmul(acc[pair + t][:, 0:N], x_part[:, k0 + k, t * P:(t + 1) * P], w_part[:, k, 0:N],
                                     start=first, stop=last)

                if n == 0:
                    for t in range(NT):
                        for k in range(2):
                            product(hi, wh, t, k, first=k == 0)
                    pe.wait_ge(s_lo, 1)
                    for t in range(NT):
                        for k in range(2):
                            product(hi, wl, t, k)
                elif n < DEPTH * NCH - 1:
                    for t in range(NT):
                        for k in range(2):
                            product(hi, wh, t, k, first=first and k == 0)
                            product(hi, wl, t, k)
                else:
                    for t in range(NT):
                        for k in range(2):
                            product(hi, wh, t, k)
                            product(hi, wl, t, k)
                            mm = product(lo, wh, t, k, last=k == 1)
                        mm.then_inc(s_tile if t < NT - 1 else s_ch, 1)
                    return
                if src:
                    pe.wait_ge(read_dve.sem, read_dve.at(l, ("pair", src)))
                for t in range(NT):
                    for k in range(2):
                        mm = product(lo, wh, t, k, last=last and k == 1)
                mm.then_inc(s_ch, 1)

            def pair(l, step):
                (what, kp), b = step[1], banks_of(step)[0]
                bank_free(l, step)
                if what == "x":
                    if l:
                        pe.wait_ge(dve_acc.sem, dve_acc.at(l - 1, ("xadd", ("down", kp // 2))))
                    else:
                        pe.wait_ge(s_ident, 16)
                        pe.wait_ge(s_x[kp], 16)
                if what == "f":
                    pe.wait_ge(dve_acc.sem, dve_acc.at(l, ("xadd", ("out", kp // 2))))
                if what == "m":
                    pe.wait_ge(merged_done.sem, merged_done.at(l, ("merge", (3, kp // 2))))
                if what == "o":
                    ev = read_dve if kp in (1, 2) else read_act
                    pe.wait_ge(ev.sem, ev.at(l, ("o", "ABCD"[kp])))
                    if kp == 1:
                        pe.wait_ge(pool_done.sem, pool_done.at(l, ("subln", None)))
                if what == "h":
                    pe.wait_ge(dve_acc.sem, dve_acc.at(l, ("act", kp)))
                for k in range(2):
                    for t in range(NT):
                        col = slice((2 * kp + k) * P, (2 * kp + k + 1) * P)
                        src = {"x": xs, "f": xs, "m": merged, "o": osb}.get(what)
                        src = hid[:, kp % 2, t, k * P:(k + 1) * P] if what == "h" else src[:, t, col]
                        mm = pe.transpose(att[:, b, (2 * k + t) * P:(2 * k + t + 1) * P], src, ident)
                mm.then_inc(att_done.now(step), 1)

            def qk(l, step):
                name = step[1]
                bank_free(l, step)
                if name[0] == "A":
                    pe.wait_ge(proj_out.sem, proj_out.at(l, ("proj", 0)))
                elif name == "Dc":
                    pe.wait_ge(act_misc.sem, act_misc.at(l, ("ngate", None)))
                else:
                    pe.wait_ge(pool_done.sem, pool_done.at(l, ("prep", name[0])))
                c0 = {"Aq": SBQ, "Ak": SBQ + MIX, "Bq": DFQ, "Bk": DFK, "Cq": MBQ, "Ck": MBK,
                      "Dq": NSQ}.get(name)
                for m in range(2):
                    for t in range(NT):
                        if name == "Dk":
                            src = kdup[:, t, 2 * m:2 * m + 2, :]
                        elif name == "Dc":
                            src = kcdup[:, t, m, :, :]
                        else:
                            src = proj[:, t, c0 + m * P:c0 + (m + 1) * P]
                        mm = pe.transpose(att[:, TP, (2 * m + t) * P:(2 * m + t + 1) * P], src, ident)
                mm.then_inc(att_done.now(step), 1)

            def causal(b, mask, buf, r, q, k, swap=False):
                pe.matmul(att[:, b, :].rearrange("p (s c) -> p s c", c=P)[:, 0:3:2, :], ident16,
                          mask.unsqueeze(1).to_broadcast([P, 2, P]), start=True, stop=False, skip_group_check=True)
                still, move = (k, q) if swap else (q, k)
                first, second = ((0, 2 * P), (P, 2 * P)) if swap else ((0, P), (0, 2 * P))
                at = 0
                for t, (c0, c1) in enumerate((first, second)):
                    for a_, b_ in ((qk_hi, qk_hi), (qk_hi, qk_lo), (qk_lo, qk_hi)):
                        mm = pe.matmul(att[:, b, at:at + c1 - c0], a_[buf][r, still, t * P:(t + 1) * P],
                                       b_[buf][r, move, c0:c1], start=False, stop=t == 1 and a_ is qk_lo,
                                       skip_group_check=True)
                    at += c1 - c0
                return mm

            def scores(l, step):
                kind, a = step
                bank_free(l, step)
                if kind == "z":
                    r = slice(64 * (a % 2), 64 * (a % 2) + 64)
                    if a == 0:
                        pe.wait_ge(read_dve.sem, read_dve.at(l, ("qk", "Ak")))
                        if l == 0:
                            pe.wait_ge(s_mask16, 1)
                    mm = causal(S0 + a % 2, mask_a, 0, r, a // 2, 2 + a // 2, swap=True)
                    mm.then_inc(att_done.now(step), 1)
                    return
                mixer, h = a
                if h == 0:
                    pe.wait_ge(read_dve.sem, read_dve.at(l, ("qk", mixer + "k")))
                if mixer == "B":
                    for m in range(2):
                        r = slice(64 * (h % 2) + 32 * m, 64 * (h % 2) + 32 * m + 32)
                        mm = causal(S0 + m, mask_s, 1, r, h // 2, 2 + h // 2)
                elif mixer == "C":
                    r = slice(64 * (h % 2), 64 * (h % 2) + 64)
                    mm = causal(S0 + h % 2, mask_s, 0, r, h // 2, 2 + h // 2)
                else:
                    m, h = h % 2, h // 2
                    r = slice(64 * (h % 2), 64 * (h % 2) + 64)
                    mm = causal(S0 + m, mask_s, 1, r, h // 2, 2 + m)
                mm.then_inc(att_done.now(step), 1)

            def cumulate(l, step):
                h = step[1]
                b = S0 + h % 2
                pe.wait_ge(dve_misc.sem, dve_misc.at(l, ("sp", h)))
                for i in range(2):
                    part = sp_parts[h % 2][:, i, :]
                    pe.matmul(att[:, b, 0:384], tri_r[:, 0, :], part, start=False, stop=False, skip_group_check=True)
                    mm = pe.matmul(att[:, b, P:2 * P], tri_r[:, 1, :], part[:, 256:384], start=False, stop=i == 1,
                                   skip_group_check=True)
                mm.then_inc(att_done.now(step), 1)

            def transpose_p(l, step):
                bank_free(l, step)
                if step[0] == "cpt":
                    pe.wait_ge(dve_misc.sem, dve_misc.at(l, ("cp", None)))
                    for t in range(NT):
                        mm = pe.transpose(att[:, TP, t * P:(t + 1) * P], cpb[:, t, :, :], ident)
                else:
                    mixer, m = step[1]
                    e = 2 * (m % 2) if mixer == "B" else m % 4
                    if mixer == "C":
                        pe.wait_ge(read_act.sem, read_act.at(l, ("sm", step[1])))
                    else:
                        pe.wait_ge(dve_misc.sem, dve_misc.at(l, ("p", step[1])))
                    for s in range(3):
                        mm = pe.transpose(att[:, TP, s * P:(s + 1) * P], eb[:, e, s * P:(s + 1) * P], ident)
                mm.then_inc(att_done.now(step), 1)

            def times_v(l, step):
                mixer, m = step[1]
                src = ("cum", m) if mixer == "A" else ("pt", (mixer, m))
                pe.wait_ge(read_act.sem, read_act.at(l, src))
                pb = PT_STEPS.index(src) % 2
                h = m // 2 if mixer == "D" else m
                v0 = {"A": SBV + h * HD, "B": DFV + h * HD, "C": MBV + h * HD}.get(mixer, (NVS, NVW)[m % 2])
                if mixer == "A":
                    pe.wait_ge(proj_out.sem, proj_out.at(l, ("proj", 1)))
                if m == 0 and mixer != "D":
                    bank_free(l, ("o", mixer))
                own = mixer != "D"
                for t in range(NT):
                    dst = att[:, OB, t * MIX + h * HD:t * MIX + (h + 1) * HD]
                    for s in range(t + 1):
                        mm = pe.matmul(dst, ptb[:, pb, (t + s) * P:(t + s + 1) * P], proj[:, s, v0:v0 + HD],
                                       start=own and s == 0, stop=s == t, skip_group_check=True)
                mm.then_inc(att_done.now(step), 1)

            def compress(l, step):
                bank_free(l, step)
                pe.wait_ge(dve_misc.sem, dve_misc.at(l, ("cbuild", None)))
                pe.wait_ge(s_cw, 16 * (l + 1))
                m, b = (0, S0) if step[0] == "ck" else (1, S1)
                for j in range(CMP_STRIDE):
                    mm = pe.matmul(att[0:16, b, 0:HD], cblk[:, m, j, :], cw[:, m, j, :],
                                   start=j == 0, stop=j == CMP_STRIDE - 1)
                mm.then_inc(att_done.now(step), 1)

            def warm_up(products):
                for _ in range(products):
                    pe.matmul(att[:, OB, :], warm[:, 0:P], warm[:, :], start=True, stop=True)

            pe.wait_ge(s_warm, 1)
            warm_up(WARM_UP[0])
            for l in range(DEPTH):
                for u in range(NCH):
                    for ll, step in steps_at(l, u):
                        kind, a = step
                        if kind == "pair":
                            pair(ll, step)
                            if step == ("pair", ("x", 0)) and ll == 0:
                                warm_up(WARM_UP[1])
                        elif kind == "qk":
                            qk(l, step)
                        elif kind in ("z", "sm"):
                            scores(l, step)
                        elif kind == "cum":
                            cumulate(l, step)
                        elif kind in ("pt", "cpt"):
                            transpose_p(l, step)
                        elif kind == "pv":
                            times_v(l, step)
                        elif kind in ("ck", "cv"):
                            compress(l, step)
                        elif kind == "cr":
                            bank_free(l, step)
                            pe.wait_ge(read_dve.sem, read_dve.at(l, ("cv", None)))
                            pe.matmul(att[:, TP, 0:HD], cst[0:16, C_REP:C_REP + P], vcs[:, :], start=True, stop=True
                                      ).then_inc(att_done.now(step), 1)
                        elif kind == "kct":
                            bank_free(l, step)
                            pe.wait_ge(pool_done.sem, pool_done.at(l, ("kcprep", None)))
                            pe.transpose(att[:, TP, 0:16], kcs[:, :, :], ident[0:16, 0:16]
                                         ).then_inc(att_done.now(step), 1)
                        elif kind == "cs":
                            bank_free(l, step)
                            pe.wait_ge(read_dve.sem, read_dve.at(l, ("kct", None)))
                            for h in range(H):
                                r = slice(64 * (h % 2), 64 * (h % 2) + 64)
                                for t in range(NT):
                                    at, q = (2 * t + h // 2) * 32, (r, h // 2, slice(t * P, (t + 1) * P))
                                    pe.matmul(att[:, S0 + h % 2, at:at + 32], qk_hi[1][q],
                                              kc_hl[r, :, :], start=True, stop=False)
                                    mm = pe.matmul(att[:, S0 + h % 2, at:at + 16], qk_lo[1][q],
                                                   kc_hl[r, 0, :], start=False, stop=True)
                            mm.then_inc(att_done.now(step), 1)
                        elif kind == "cpv":
                            bank_free(l, ("o", "D"))
                            pe.wait_ge(read_act.sem, read_act.at(l, ("cpt", None)))
                            pe.wait_ge(read_dve.sem, read_dve.at(l, ("cr", None)))
                            for t in range(NT):
                                mm = pe.matmul(att[:, OB, t * MIX:(t + 1) * MIX], ptc[:, t, :], vblk[:, :, :],
                                               start=t == 0, stop=True, skip_group_check=True)
                            mm.then_inc(att_done.now(step), 1)
                    products(l, u)

        @block.scalar
        def _(act):
            copy = ACT.Copy

            def split(n):
                if n >= DEPTH * NCH:
                    return
                if n >= WR:
                    act.wait_ge(s_ch, n - WR + 1)
                act.wait_ge(s_raw[n % RAW], raw_value(n))
                N = width(n % NCH)
                act.activation(w_hi[:, n % WR, :, 0:N], w_raw[:, n % RAW, :, 0:N], copy).then_inc(s_hi, 1)

            def pair_hi(l, step):
                (what, kp), b = step[1], banks_of(step)[0]
                act.wait_ge(att_done.sem, att_done.at(l, step))
                if what in "mf" or (what == "x" and l):
                    act.wait_ge(s_ch, {"x": chunk(l - 1, U_DOWN), "m": chunk(l, U_BR),
                                       "f": chunk(l, CHUNKS.index(("out", kp, 1)) + 1)}[what])
                dst = {"o": ot_hi, "h": ht_hi}.get(what, xt_hi)
                if what in "xf":
                    if l == 0 or what == "x":
                        act.wait_ge(s_gt, 16 * (l + 1))
                    for k in range(2):
                        g = gt[:, 2 * kp + k + (KT if what == "f" else 0):][:, 0:1]
                        ins = act.activation(dst[:, 2 * kp + k, :], att[:, b, k * SEQ:(k + 1) * SEQ], copy, scale=g)
                else:
                    ins = act.activation(dst[:, 2 * kp:2 * kp + 2, :].rearrange("p k t -> p (k t)"), att[:, b, :], copy)
                ins.then_inc(hi_done.now(step), 1)

            def qk_copy(l, step):
                name = step[1]
                act.wait_ge(att_done.sem, att_done.at(l, step))
                if name == "Dc":
                    if l:
                        act.wait_ge(dve_misc.sem, dve_misc.at(l - 1, ("cbuild", None)))
                    act.activation(kcvt[:, :, :].rearrange("p m t -> p (m t)"), att[:, TP, :], copy
                                   ).then_inc(read_act.now(step), 1)
                    return
                m = 0 if name[1] == "q" else 2
                act.activation(qk_hi[name[0] in "BD"][:, m:m + 2, :].rearrange("p m t -> p (m t)"), att[:, TP, :], copy,
                               scale=HD ** -0.5 if name == "Aq" else 1.0).then_inc(hi_done.now(step), 1)

            def e_free(l, step):
                mine = e_of(step)[0]
                uses = [s for s in E_STEPS if set(e_of(s)[0]) & set(mine)]
                for e in mine:
                    prev = previous(l, [s for s in uses if e in e_of(s)[0]], step)
                    if prev:
                        act.wait_ge(att_done.sem, att_done.at(prev[0], e_of(prev[1])[1]))

            def pt_free(l, step):
                n = l * len(PT_STEPS) + PT_STEPS.index(step) - 2
                if n >= 0:
                    act.wait_ge(att_done.sem, att_done.at(n // len(PT_STEPS), pv_step(PT_STEPS[n % len(PT_STEPS)])))
                return PT_STEPS.index(step) % 2

            def exps(l, step):
                mixer, m = step[1]
                scale = (DD if mixer == "B" else HD) ** -0.5
                r = keys("sm").index(step) % 2
                act.wait_ge(att_done.sem, att_done.at(l, step))
                act.wait_ge(dve_misc.sem, dve_misc.at(l, step))
                e_free(l, step)
                maps = 2 if mixer == "B" else 1
                for i in range(maps):
                    b = banks_of(step)[i]
                    e = e_of(step)[0][i]
                    for t, cols in enumerate((slice(0, P), slice(P, 384))):
                        j = maps * t + i
                        ins = act.activation(eb[:, e, cols], att[:, b, cols], ACT.Exp, scale=scale,
                                             bias=nbias[r][:, j:j + 1], accum_out=sums[r][:, j:j + 1])
                ins.then_inc(read_act.now(step), 1)

            softplus_chain = [0]

            def do(l, step):
                kind, a = step
                if kind == "proj":
                    act.wait_ge(s_ch, chunk(l, 4 * a + 4))
                    if a == 0:
                        act.wait_ge(pool_done.sem, pool_done.at(l, ("stats", "x")))
                    N = in_cols(a)
                    for t in range(NT):
                        ins = act.activation(proj[:, t, a * NC:a * NC + N], acc[bank_pair(l, step) + t][:, 0:N],
                                             copy, scale=xr["x"][:, t:t + 1])
                    ins.then_inc(proj_out.now(step), 1)
                elif kind == "act":
                    act.wait_ge(s_ch, chunk(l, U_FFN + 4 * a + 4))
                    if a == 0:
                        act.wait_ge(pool_done.sem, pool_done.at(l, ("stats", "f")))
                    else:
                        act.wait_ge(dve_acc.sem, dve_acc.at(l, ("act", a - 1)))
                    for t in range(NT):
                        ins = act.activation(silu[:, t, :], acc[bank_pair(l, step) + t][:, 0:FC], ACT.Silu,
                                             scale=xr["f"][:, t:t + 1])
                    ins.then_inc(act_misc.now(step), 1)
                elif kind == "pair":
                    pair_hi(l, step)
                elif kind == "stats":
                    if a == "x" and l == 0:
                        for landed in s_x:
                            act.wait_ge(landed, 16)
                    else:
                        prev = (l - 1, ("xadd", ("down", 1))) if a == "x" else (l, ("xadd", ("out", 1)))
                        act.wait_ge(dve_acc.sem, dve_acc.at(*prev))
                    for t in range(NT):
                        ins = act.activation(osb[:, t, :], xs[:, t, :], ACT.Square, accum_out=xss[:, t:t + 1])
                    ins.then_inc(act_misc.now(step), 1)
                elif kind == "lambda":
                    act.wait_ge(lam_sums.sem, lam_sums.at(l, step))
                    act.activation(lexp, lsum, ACT.Exp).then_inc(act_misc.now(step), 1)
                elif kind == "qk":
                    qk_copy(l, step)
                elif kind == "z":
                    act.wait_ge(att_done.sem, att_done.at(l, step))
                    e_free(l, step)
                    t1 = eb[:, 2 * (a % 2), :]
                    for f, kw in ((ACT.Abs, {}), (ACT.Exp, {"scale": -1.0}), (ACT.Ln, {"bias": 1.0})):
                        ins = act.activation(t1, att[:, S0 + a % 2, 0:384] if f == ACT.Abs else t1, f, **kw)
                        ins.then_inc(s_zc, 1)
                        softplus_chain[0] += 1
                        if f != ACT.Ln:
                            act.wait_ge(s_zc, softplus_chain[0])
                elif kind == "cum":
                    act.wait_ge(att_done.sem, att_done.at(l, step))
                    pb = pt_free(l, step)
                    act.activation(ptb[:, pb, :], att[:, S0 + a % 2, 0:384], ACT.Exp
                                   ).then_inc(read_act.now(step), 1)
                elif kind == "sm":
                    exps(l, step)
                elif kind == "pt":
                    act.wait_ge(att_done.sem, att_done.at(l, step))
                    pb = pt_free(l, step)
                    act.activation(ptb[:, pb, :], att[:, TP, 0:384], copy).then_inc(read_act.now(step), 1)
                elif kind == "cpt":
                    act.wait_ge(att_done.sem, att_done.at(l, step))
                    if l:
                        act.wait_ge(att_done.sem, att_done.at(l - 1, ("cpv", None)))
                    act.activation(ptc[:, :, :].rearrange("p t q -> p (t q)"), att[:, TP, 0:SEQ], copy
                                   ).then_inc(read_act.now(step), 1)
                elif kind == "o" and a in "AD":
                    last = {"D": 2 * H - 1}.get(a, H - 1)
                    act.wait_ge(att_done.sem, att_done.at(l, ("pv", (a, last))))
                    i = "ABCD".index(a)
                    act.activation(osb[:, :, i * MIX:(i + 1) * MIX],
                                   att[:, OB, :].rearrange("p (t d) -> p t d", t=NT), copy
                                   ).then_inc(read_act.now(step), 1)
                elif kind == "prep":
                    act.wait_ge(proj_out.sem, proj_out.at(l, ("proj", {"B": 2, "C": 3, "D": 5}[a])))
                    if a != "B":
                        act.wait_ge(dve_misc.sem, dve_misc.at(l, ("prep", {"C": "B", "D": "C"}[a])))
                    if a == "D":
                        for m, c in ((0, NKS), (1, NKS), (2, NKW), (3, NKW)):
                            act.activation(kdup[:, :, m, :], proj[:, :, c:c + HD], copy)
                        act.activation(squares[:, :, 0:MIX], proj[:, :, NSQ:NSQ + MIX], ACT.Square
                                       ).then_inc(s_kd, 1)
                        act.wait_ge(s_kd, l + 1)
                        act.activation(squares[:, :, MIX:2 * MIX], kdup[:, :, :, :].rearrange("p t m d -> p t (m d)"),
                                       ACT.Square).then_inc(act_misc.now(step), 1)
                    else:
                        c0 = DFQ if a == "B" else MBQ
                        act.activation(squares[:, :, :], proj[:, :, c0:c0 + 2 * MIX], ACT.Square
                                       ).then_inc(act_misc.now(step), 1)
                elif kind == "ngate":
                    act.activation(ng.rearrange("p (t g) -> p t g", t=NT), proj[:, :, NGT:NGT + 3 * H], ACT.Exp,
                                   scale=-1.0)
                    for m in range(2):
                        src = proj[:, :, NKC + m * HD:NKC + (m + 1) * HD]
                        ins = act.activation(kcdup[:, :, m, :, :], src.unsqueeze(2).to_broadcast([P, NT, 2, HD]), copy)
                    ins.then_inc(act_misc.now(step), 1)
                elif kind == "ck":
                    act.wait_ge(att_done.sem, att_done.at(l, step))
                    for m in range(2):
                        ins = act.activation(kcs[:, m, :], att[0:16, S0, 0:HD], copy)
                    ins.then_inc(read_act.now(step), 1)
                elif kind == "kcprep":
                    act.wait_ge(read_act.sem, read_act.at(l, ("ck", None)))
                    act.activation(kcsq[:, :, :], kcs[:, :, :], ACT.Square).then_inc(act_misc.now(step), 1)
                elif kind == "kct":
                    act.wait_ge(att_done.sem, att_done.at(l, step))
                    act.activation(kc_hl[:, 0, :], att[:, TP, 0:16], copy).then_inc(hi_done.now(step), 1)
                elif kind == "cs":
                    act.wait_ge(cs_max.sem, cs_max.at(l, step))
                    act.activation(csc[:, :, :, :].rearrange("p t h n -> p (t h n)"),
                                   csc[:, :, :, :].rearrange("p t h n -> p (t h n)"), ACT.Exp, scale=HD ** -0.5
                                   ).then_inc(act_misc.now(step), 1)
                elif kind == "sig":
                    act.wait_ge(dve_acc.sem, dve_acc.at(l, ("zg", 2 * a + 1)))
                    act.activation(zg[:, :, a, :], zg[:, :, a, :], ACT.Sigmoid).then_inc(act_misc.now(step), 1)

            act.wait_ge(s_phalf, 1)
            act.activation(sm(240, 2), half[:, 0:2], copy)
            for l in range(DEPTH):
                for u in range(NCH + 1):
                    todo = steps_at(l, u)
                    for n, (ll, step) in enumerate(todo):
                        if rank(step) < 3:
                            do(ll, step)
                        if l == u == 0 and n < LEAD:
                            split(n)
                    if u == NCH:
                        continue
                    split(chunk(l, u) + LEAD)
                    if l == 0 and u == 6:
                        act.wait_ge(s_mask, 16)
                        act.activation(cst16[:, P:], masks32, copy)
                        act.activation(ident16, ident, copy)
                        act.wait_ge(s_const, 16)
                        act.activation(tri_r[:, :, :].rearrange("p i k -> p (i k)"), cst[:, C_TRI:C_TRI + 2 * P], copy
                                       ).then_inc(s_mask16, 1)
                    for ll, step in todo:
                        if rank(step) >= 3:
                            do(ll, step)

        @block.vector
        def _(dve):
            chain = [0]

            def settled(ins):
                ins.then_inc(s_dve, 1)
                chain[0] += 1
                dve.wait_ge(s_dve, chain[0])

            def split(n):
                if n >= DEPTH * NCH:
                    return
                dve.wait_ge(s_hi, n + 1)
                N = width(n % NCH)
                dve.tensor_tensor(w_lo[:, n % WR, :, 0:N], w_raw[:, n % RAW, :, 0:N],
                                  w_hi[:, n % WR, :, 0:N].bitcast(F32), ALU.subtract).then_inc(s_lo, 1)

            def pair_lo(l, step):
                (what, kp), b = step[1], banks_of(step)[0]
                dve.wait_ge(hi_done.sem, hi_done.at(l, step))
                hi, lo = {"o": (ot_hi, ot_lo), "h": (ht_hi, ht_lo)}.get(what, (xt_hi, xt_lo))
                if what in "xf":
                    for k in range(2):
                        g = gt[:, 2 * kp + k + (KT if what == "f" else 0):][:, 0:1]
                        ins = dve.scalar_tensor_tensor(out=lo[:, 2 * kp + k, :], in0=att[:, b, k * SEQ:(k + 1) * SEQ],
                                                       scalar=g, in1=hi[:, 2 * kp + k, :].bitcast(F32),
                                                       op0=ALU.mult, op1=ALU.subtract)
                else:
                    ins = dve.tensor_tensor(lo[:, 2 * kp:2 * kp + 2, :].rearrange("p k t -> p (k t)"), att[:, b, :],
                                            hi[:, 2 * kp:2 * kp + 2, :].rearrange("p k t -> p (k t)").bitcast(F32),
                                            ALU.subtract)
                ins.then_inc(read_dve.now(step), 1)

            dve.memset(warm[:, :], 0.0).then_inc(s_warm, 1)
            dve.memset(cblk[:, :, :, :], 0.0).then_inc(s_init, 1)
            dve.memset(vblk[:, :, :], 0.0).then_inc(s_init, 1)
            dve.memset(cpb[:, :, :, :], 0.0).then_inc(s_init, 1)
            dve.wait_ge(s_init, 3)
            def do(l, step):
                kind, a = step
                if kind == "zg":
                    dve.wait_ge(s_ch, chunk(l, U_GATE + 4 * a + 4))
                    i, c = divmod(a, 2)
                    dve.wait_ge(s_bg[i % 2], 16 * (2 * l + i // 2 + 1))
                    for t in range(NT):
                        ins = dve.scalar_tensor_tensor(
                            out=zg[:, t, i, c * NC:(c + 1) * NC], in0=acc[bank_pair(l, step) + t][:, :],
                            scalar=xr["x"][:, t:t + 1], in1=bg[:, i % 2, c * NC:(c + 1) * NC],
                            op0=ALU.mult, op1=ALU.add)
                    ins.then_inc(dve_acc.now(step), 1)
                elif kind == "merge":
                    i, c = a
                    dve.wait_ge(s_ch, chunk(l, U_BR + 4 * c + i + 1))
                    dve.wait_ge(act_misc.sem, act_misc.at(l, ("sig", i)))
                    cols, half_ = slice(c * NC, (c + 1) * NC), slice((i % 2) * NC, (i % 2 + 1) * NC)
                    before = {(2, 1): (2, 0), (3, 0): (1, 0), (3, 1): (1, 1)}.get(a)
                    if before:
                        dve.wait_ge(pool_done.sem, pool_done.at(l, ("merge", before)))
                    for t in range(NT):
                        ins = dve.tensor_tensor(merged[:, t, cols] if i == 0 else prod[:, t, half_],
                                                acc[bank_pair(l, step) + t][:, :], zg[:, t, i, cols], ALU.mult)
                    ins.then_inc(dve_acc.now(step), 1)
                    if i == 3:
                        dve.wait_ge(dve_acc.sem, dve_acc.at(l, step))
                        dve.wait_ge(pool_done.sem, pool_done.at(l, ("merge", (2, c))))
                        for t in range(NT):
                            ins = dve.tensor_tensor(merged[:, t, cols], merged[:, t, cols], prod[:, t, half_], ALU.add)
                        ins.then_inc(merged_done.now(step), 1)
                elif kind == "xadd":
                    what, c = a
                    first_tile = 0
                    if l == DEPTH - 1 and a == ("down", 1):
                        dve.wait_ge(s_tile, 1)
                        first_tile, cols = 1, slice(NC, 2 * NC)
                        dve.tensor_tensor(xs[:, 0, cols], acc[bank_pair(l, step)][:, :], xs[:, 0, cols], ALU.add
                                          ).then_inc(s_tsum, 1)
                    dve.wait_ge(s_ch, chunk(l, CHUNKS.index(("out", 3, c) if what == "out" else ("down", N_DOWN - 1, c)) + 1))
                    cols = slice(c * NC, (c + 1) * NC)
                    for t in range(first_tile, NT):
                        ins = dve.tensor_tensor(xs[:, t, cols], acc[bank_pair(l, step) + t][:, :], xs[:, t, cols], ALU.add)
                    ins.then_inc(dve_acc.now(step), 1)
                elif kind == "act":
                    dve.wait_ge(act_misc.sem, act_misc.at(l, step))
                    if a >= 2:
                        dve.wait_ge(att_done.sem, att_done.at(l, ("pair", ("h", a - 2))))
                    for t in range(NT):
                        ins = dve.scalar_tensor_tensor(
                            out=hid[:, a % 2, t, :], in0=acc[bank_pair(l, step) + t][:, FC:2 * FC],
                            scalar=xr["f"][:, t:t + 1], in1=silu[:, t, :], op0=ALU.mult, op1=ALU.mult)
                    ins.then_inc(dve_acc.now(step), 1)
                elif kind == "pair":
                    pair_lo(l, step)
                elif kind == "qk" and a != "Dc":
                    dve.wait_ge(hi_done.sem, hi_done.at(l, step))
                    m = 0 if a[1] == "q" else 2
                    hi, lo = (v[a[0] in "BD"][:, m:m + 2, :].rearrange("p m t -> p (m t)") for v in (qk_hi, qk_lo))
                    if a == "Aq":
                        ins = dve.scalar_tensor_tensor(out=lo, in0=att[:, TP, :], scalar=HD ** -0.5,
                                                       in1=hi.bitcast(F32), op0=ALU.mult, op1=ALU.subtract)
                    else:
                        ins = dve.tensor_tensor(lo, att[:, TP, :], hi.bitcast(F32), ALU.subtract)
                    ins.then_inc(read_dve.now(step), 1)
                elif kind == "kct":
                    dve.wait_ge(hi_done.sem, hi_done.at(l, step))
                    dve.tensor_tensor(kc_hl[:, 1, :], att[:, TP, 0:16], kc_hl[:, 0, :].bitcast(F32), ALU.subtract
                                      ).then_inc(read_dve.now(step), 1)
                elif kind == "lambda":
                    dve.wait_ge(s_small, 48 * (l + 1))
                    lv = lamb[:, :, :].rearrange("p (a b) d -> p a b d", b=2)
                    lp = rot_l[:, :].rearrange("p (a d) -> p a d", a=2)
                    settled(dve.tensor_tensor(lp, lv[:, :, 0, :], lv[:, :, 1, :], ALU.mult))
                    dve.tensor_reduce(lsum, lp, AX.X, ALU.add).then_inc(lam_sums.now(step), 1)
                    dve.wait_ge(act_misc.sem, act_misc.at(l, step))
                    settled(dve.tensor_tensor(nlam, lexp[:, 1:2], lexp[:, 0:1], ALU.subtract))
                    dve.tensor_scalar(nlam, nlam, -lam_init(l), None, ALU.add).then_inc(dve_misc.now(step), 1)
                elif kind == "prep":
                    dve.wait_ge(act_misc.sem, act_misc.at(l, step))
                    d = DD if a == "B" else HD
                    n = NT * 2 * MIX // d
                    prev = {"B": ("prep", "D"), "C": ("prep", "B"), "D": ("prep", "C")}[a]
                    if l or a != "B":
                        dve.wait_ge(pool_done.sem, pool_done.at(l - (a == "B"), prev))
                    dve.tensor_reduce(ss[:, 0:n], squares[:, :, :].rearrange("p t (u d) -> p (t u) d", d=d),
                                      AX.X, ALU.add).then_inc(dve_misc.now(step), 1)
                elif kind == "kcprep":
                    dve.wait_ge(act_misc.sem, act_misc.at(l, step))
                    dve.tensor_reduce(kcss, kcsq[:, :, :], AX.X, ALU.add).then_inc(dve_misc.now(step), 1)
                elif kind == "subln":
                    dve.wait_ge(sub_sq.sem, sub_sq.at(l, step))
                    dve.tensor_reduce(obss, osq[:, :, :].rearrange("p t (h d) -> p (t h) d", d=HD),
                                      AX.X, ALU.add).then_inc(dve_misc.now(step), 1)
                elif kind == "sp":
                    dve.wait_ge(s_zc, 3 * (l * H + a + 1))
                    t1, t2 = eb[:, 2 * (a % 2), :], eb[:, 2 * (a % 2) + 1, :]
                    settled(dve.scalar_tensor_tensor(out=t2, in0=att[:, S0 + a % 2, 0:384], scalar=0.0, in1=t1,
                                                     op0=ALU.max, op1=ALU.add))
                    hi, lo = (sp_parts[a % 2][:, i, :] for i in range(2))
                    settled(dve.tensor_copy(hi, t2))
                    dve.tensor_tensor(lo, t2, hi.bitcast(F32), ALU.subtract).then_inc(dve_misc.now(step), 1)
                elif kind == "sm":
                    mixer, m = a
                    r = keys("sm").index(step) % 2
                    b, maps = banks_of(step)[0], len(banks_of(step))
                    dve.wait_ge(att_done.sem, att_done.at(l, step))
                    dve.tensor_reduce(stat[r][:, 0:maps], att[:, b:b + maps, 0:P], AX.X, ALU.max)
                    settled(dve.tensor_reduce(stat[r][:, maps:2 * maps], att[:, b:b + maps, P:384], AX.X, ALU.max))
                    dve.tensor_scalar(nbias[r][:, 0:2 * maps], stat[r][:, 0:2 * maps],
                                      -(DD if mixer == "B" else HD) ** -0.5, None, ALU.mult
                                      ).then_inc(dve_misc.now(step), 1)
                elif kind == "p":
                    mixer, m = a
                    r = keys("sm").index(("sm", a)) % 2
                    e = e_of(("sm", a))[0][0]
                    dve.wait_ge(read_act.sem, read_act.at(l, ("sm", a)))
                    if mixer == "B":
                        sum_, c_ = (v[r].rearrange("p (t m) -> p m t", m=2) for v in (sums, coef))
                        dve.reciprocal(row["B"][:, :, m], sum_[:, 0, :])
                        settled(dve.reciprocal(c_[:, 1, :], sum_[:, 1, :]))
                        settled(dve.scalar_tensor_tensor(out=c_[:, 1, :], in0=sum_[:, 0, :], scalar=nlam,
                                                         in1=c_[:, 1, :], op0=ALU.mult, op1=ALU.mult))
                        for t, cols in enumerate((slice(0, P), slice(P, 384))):
                            ins = dve.scalar_tensor_tensor(out=eb[:, e, cols], in0=eb[:, e + 1, cols],
                                                           scalar=c_[:, 1, t:t + 1], in1=eb[:, e, cols],
                                                           op0=ALU.mult, op1=ALU.add)
                    elif mixer == "C":
                        ins = dve.reciprocal(row["C"][:, :, m], sums[r][:, 0:2])
                    else:
                        settled(dve.reciprocal(coef[r][:, 0:2], sums[r][:, 0:2]))
                        gv = ng.rearrange("p (t j h) -> p j h t", t=NT, j=3)[:, 1 + m % 2, m // 2, :]
                        settled(dve.tensor_tensor(coef[r][:, 0:2], coef[r][:, 0:2], gv, ALU.mult))
                        for t, cols in enumerate((slice(0, P), slice(P, 384))):
                            ins = dve.tensor_scalar(eb[:, e, cols], eb[:, e, cols], coef[r][:, t:t + 1], None, ALU.mult)
                    ins.then_inc(dve_misc.now(step), 1)
                elif kind == "o" and a in "BC":
                    dve.wait_ge(att_done.sem, att_done.at(l, ("pv", (a, H - 1))))
                    dve.wait_ge(dve_misc.sem, dve_misc.at(l, ("p", (a, H - 1))))
                    i = "ABCD".index(a)
                    dve.tensor_tensor(osb[:, :, i * MIX:(i + 1) * MIX].rearrange("p t (h d) -> p t h d", d=HD),
                                      att[:, OB, :].rearrange("p (t h d) -> p t h d", t=NT, d=HD),
                                      row[a].unsqueeze(3).to_broadcast([P, NT, H, HD]), ALU.mult
                                      ).then_inc(read_dve.now(step), 1)
                elif kind == "ngate":
                    dve.wait_ge(act_misc.sem, act_misc.at(l, step))
                    settled(dve.tensor_scalar(ng, ng, 1.0, None, ALU.add))
                    dve.reciprocal(ng, ng).then_inc(dve_misc.now(step), 1)
                elif kind == "cbuild":
                    dve.wait_ge(read_act.sem, read_act.at(l, ("qk", "Dc")))
                    kv = kcvt[:, :, :].rearrange("p m (n j) -> p m j n", j=CMP_STRIDE)
                    for half_ in range(2):
                        r = slice(half_ * HD, (half_ + 1) * HD)
                        for m in range(2):
                            ins = dve.tensor_tensor(cblk[r, m, :, 0:NCMP], kv[r, m, :, half_:half_ + NCMP],
                                                    pet[r, m, :].unsqueeze(2).to_broadcast([HD, CMP_STRIDE, NCMP]), ALU.add)
                    ins.then_inc(dve_misc.now(step), 1)
                elif kind == "cv":
                    dve.wait_ge(att_done.sem, att_done.at(l, step))
                    dve.tensor_copy(vcs[:, :], att[0:16, S1, 0:HD]).then_inc(read_dve.now(step), 1)
                elif kind == "cr":
                    dve.wait_ge(att_done.sem, att_done.at(l, step))
                    for h in range(H):
                        r = slice(32 * h, 32 * h + 32)
                        ins = dve.tensor_copy(vblk[r, h, :], att[r, TP, 0:HD])
                    ins.then_inc(read_dve.now(step), 1)
                elif kind == "cs":
                    dve.wait_ge(att_done.sem, att_done.at(l, step))
                    hv = csc[:, :, :, :].rearrange("p t (a b) n -> p t b a n", b=2)
                    sc = att[:, S0:S0 + 2, 0:NT * 64].rearrange("p b (t a n) -> p t b a n", t=NT, a=2)
                    for t in range(NT):
                        ins = dve.tensor_tensor(hv[:, t], sc[:, t, :, :, 0:16], cmask[:, t, :].unsqueeze(1).unsqueeze(1)
                                                .to_broadcast([P, 2, 2, 16]), ALU.add)
                    settled(ins)
                    for t in range(NT):
                        ins = dve.tensor_tensor(hv[:, t], sc[:, t, :, :, 16:32], hv[:, t], ALU.add)
                    ins.then_inc(read_dve.now(step), 1)
                    dve.wait_ge(read_dve.sem, read_dve.at(l, step))
                    flat = csc[:, :, :, :].rearrange("p t h n -> p (t h) n")
                    settled(dve.tensor_reduce(cmx, flat, AX.X, ALU.max))
                    dve.tensor_tensor(flat, flat, cmx.unsqueeze(2).to_broadcast([P, 8, 16]), ALU.subtract
                                      ).then_inc(cs_max.now(step), 1)
                elif kind == "cp":
                    dve.wait_ge(act_misc.sem, act_misc.at(l, ("cs", None)))
                    flat = csc[:, :, :, :].rearrange("p t h n -> p (t h) n")
                    settled(dve.tensor_tensor(csc[:, :, :, :], csc[:, :, :, :],
                                              czero.unsqueeze(2).to_broadcast([P, NT, H, 16]), ALU.mult))
                    settled(dve.tensor_reduce(csum, flat, AX.X, ALU.add))
                    settled(dve.tensor_scalar(csum, csum, 1e-30, None, ALU.max))
                    settled(dve.reciprocal(csum, csum))
                    g0 = ng.rearrange("p (t j h) -> p t j h", t=NT, j=3)[:, :, 0, :]
                    c8 = csum.rearrange("p (t h) -> p t h", t=NT)
                    settled(dve.tensor_tensor(c8, c8, g0, ALU.mult))
                    dve.tensor_tensor(cpb[:, :, :, 0:16], csc[:, :, :, :],
                                      c8.unsqueeze(3).to_broadcast([P, NT, H, 16]), ALU.mult
                                      ).then_inc(dve_misc.now(step), 1)

            for l in range(DEPTH):
                for u in range(NCH + 1):
                    todo = steps_at(l, u)
                    for n, (ll, step) in enumerate(todo):
                        if rank(step) < 3:
                            do(ll, step)
                        if l == u == 0 and n < LEAD:
                            split(n)
                    if u == NCH:
                        continue
                    split(chunk(l, u) + LEAD)
                    for ll, step in todo:
                        if rank(step) >= 3:
                            do(ll, step)

        @block.gpsimd
        def _(pool):
            chain = [0]

            def settled(ins):
                ins.then_inc(s_pool, 1)
                chain[0] += 1
                pool.wait_ge(s_pool, chain[0])

            def rsqrt(dst, sumsq, n, exps_):
                settled(pool.tensor_scalar(dst, sumsq, 1.0 / n, EPS, ALU.mult, ALU.add))
                return pool.tensor_tensor(dst, dst, exps_, ALU.pow)

            def rotate(v, table, r, buf):
                h = r // 2
                a, b = buf
                cos, sin = table
                pool.tensor_tensor(a, v[..., 0:r], cos, ALU.mult)
                pool.tensor_tensor(b[..., 0:h], v[..., h:r], sin[..., 0:h], ALU.mult)
                settled(pool.tensor_tensor(b[..., h:r], v[..., 0:h], sin[..., h:r], ALU.mult))
                return pool.tensor_tensor(v[..., 0:r], a, b, ALU.add)

            def prep(v, rr, gains_, d, rope_):
                u = v.shape[2]
                settled(pool.tensor_tensor(v, v, rr.unsqueeze(3).to_broadcast([P, NT, u, d]), ALU.mult))
                n = u // len(gains_)
                for i, g in enumerate(gains_):
                    for t in range(NT):
                        ins = pool.tensor_tensor(v[:, t, i * n:(i + 1) * n, :], v[:, t, i * n:(i + 1) * n, :],
                                                 gn[:, g:g + d].unsqueeze(1).to_broadcast([P, n, d]), ALU.mult)
                settled(ins)
                r = d // 4
                for t in range(NT):
                    a = rot1[:, t * P:t * P + u * r].rearrange("p (u r) -> p u r", r=r)
                    b = rot2[:, t * P:t * P + u * r].rearrange("p (u r) -> p u r", r=r)
                    cos = rope_[:, t, 0, :].unsqueeze(1).to_broadcast([P, u, r])
                    sin = rope_[:, t, 1, :].unsqueeze(1).to_broadcast([P, u, r])
                    ins = rotate(v[:, t, :, :], (cos, sin), r, (a, b))
                return ins

            pool.memset(half, -0.5).then_inc(s_phalf, 1)
            pool.wait_ge(s_phalf, 1)
            for l in range(DEPTH):
                for u in range(NCH):
                    for step in STEPS[u]:
                        kind, a = step
                        if kind == "stats":
                            pool.wait_ge(act_misc.sem, act_misc.at(l, step))
                            rsqrt(xr[a], xss, D_MODEL, half[:, 0:NT]).then_inc(pool_done.now(step), 1)
                        elif kind == "prep":
                            pool.wait_ge(dve_misc.sem, dve_misc.at(l, step))
                            pool.wait_ge(s_small, 48 * (l + 1))
                            pool.wait_ge(s_const, 16)
                            d = DD if a == "B" else HD
                            n = NT * 2 * MIX // d
                            settled(rsqrt(rs[:, 0:n], ss[:, 0:n], d, half[:, 0:n]))
                            rr = rs[:, 0:n].rearrange("p (t u) -> p t u", t=NT)
                            if a == "D":
                                v = proj[:, :, NSQ:NSQ + MIX].rearrange("p t (u d) -> p t u d", d=HD)
                                settled(prep(v, rr[:, :, 0:H], (G_NQ,), HD, rope64))
                                ins = prep(kdup[:, :, :, :], rr[:, :, H:2 * H], (G_KS, G_KW), HD, rope64)
                            else:
                                c0 = DFQ if a == "B" else MBQ
                                v = proj[:, :, c0:c0 + 2 * MIX].rearrange("p t (u d) -> p t u d", d=d)
                                ins = prep(v, rr, (G_DQ, G_DK) if a == "B" else (G_MQ, G_MK), d,
                                           rope32 if a == "B" else rope64)
                            ins.then_inc(pool_done.now(step), 1)
                            pool.wait_ge(pool_done.sem, pool_done.at(l, step))
                        elif kind == "kcprep":
                            pool.wait_ge(dve_misc.sem, dve_misc.at(l, step))
                            settled(rsqrt(kcr, kcss, HD, half[0:16, 0:2]))
                            v = kcs[:, :, :]
                            settled(pool.tensor_tensor(v, v, kcr.unsqueeze(2).to_broadcast([16, 2, HD]), ALU.mult))
                            settled(pool.tensor_tensor(v, v, gn[0:16, G_KC:G_KC + HD].unsqueeze(1).to_broadcast([16, 2, HD]), ALU.mult))
                            r = HD // 4
                            bufs = [b[0:16, 0:2 * r].rearrange("p (u r) -> p u r", r=r) for b in (rot1, rot2)]
                            tables = [ropec[:, i, :].unsqueeze(1).to_broadcast([16, 2, r]) for i in range(2)]
                            rotate(v, tables, r, bufs).then_inc(pool_done.now(step), 1)
                            pool.wait_ge(pool_done.sem, pool_done.at(l, step))
                        elif kind == "subln":
                            pool.wait_ge(read_dve.sem, read_dve.at(l, ("o", "B")))
                            if l:
                                pool.wait_ge(dve_misc.sem, dve_misc.at(l - 1, step))
                            ob = osb[:, :, MIX:2 * MIX]
                            pool.tensor_tensor(osq[:, :, :], ob, ob, ALU.mult).then_inc(sub_sq.now(step), 1)
                            pool.wait_ge(dve_misc.sem, dve_misc.at(l, step))
                            settled(rsqrt(obr, obss, HD, half[:, 0:8]))
                            settled(pool.tensor_scalar(obr, obr, 1.0 - lam_init(l), None, ALU.mult))
                            obv = ob.rearrange("p t (h d) -> p t h d", d=HD)
                            settled(pool.tensor_tensor(obv, obv, obr.rearrange("p (t h) -> p t h", t=NT).unsqueeze(3)
                                                       .to_broadcast([P, NT, H, HD]), ALU.mult))
                            for t in range(NT):
                                ins = pool.tensor_tensor(obv[:, t, :, :], obv[:, t, :, :], gn[:, G_SUB:G_SUB + HD].unsqueeze(1)
                                                         .to_broadcast([P, H, HD]), ALU.mult)
                            ins.then_inc(pool_done.now(step), 1)
                            pool.wait_ge(pool_done.sem, pool_done.at(l, step))
                        elif kind == "merge" and a[0] in (1, 2):
                            pool.wait_ge(dve_acc.sem, dve_acc.at(l, step))
                            if a[0] == 2:
                                pool.wait_ge(pool_done.sem, pool_done.at(l, ("merge", (1, a[1]))))
                            cols, half_ = (slice(c * NC, (c + 1) * NC) for c in (a[1], a[0] % 2))
                            pool.tensor_tensor(merged[:, :, cols], merged[:, :, cols], prod[:, :, half_], ALU.add
                                               ).then_inc(pool_done.now(step), 1)


def lam_init(l):
    return 0.8 - 0.6 * math.exp(-0.3 * l)


def rope_table(positions, width):
    r = width // 4
    inv = np.float32(500000.0) ** (-np.arange(r // 2, dtype=np.float32) * np.float32(2.0) / np.float32(r))
    ang = positions.astype(np.float32)[:, None] * inv[None, :].astype(np.float32)
    c, s = np.cos(ang).astype(np.float32), np.sin(ang).astype(np.float32)
    return np.concatenate([c, c, -s, s], axis=1)


def constants():
    p = np.arange(P)
    c = np.zeros((P, C_END), np.float32)
    c[:, C_ID:C_ID + P] = np.eye(P)
    c[:, C_TRI:C_TRI + P] = -(p[:, None] >= p[None, :]).astype(np.float32)
    c[:, C_ONE:C_ONE + P] = -1.0
    pos = np.arange(SEQ)
    tile = lambda t: t.reshape(NT, P, -1).transpose(1, 0, 2).reshape(P, -1)
    c[:, C_R32:C_R32 + 32] = tile(rope_table(pos, DD))
    c[:, C_R64:C_R64 + 64] = tile(rope_table(pos, HD))
    ends = CMP_STRIDE * np.arange(16) + CMP_LEN - 1
    seen = (ends[None, :] <= pos[:, None]) & (np.arange(16)[None, :] < NCMP)
    c[:, C_CM:C_CM + 32] = tile(np.where(seen, 0.0, NEG).astype(np.float32))
    c[:, C_CZ:C_CZ + 32] = tile(seen.astype(np.float32))
    c[0:16, C_RC:C_RC + 32] = rope_table(ends, HD)
    for h in range(H):
        c[0:16, C_REP + 32 * h:C_REP + 32 * h + 16] = np.eye(16)
    strict = np.where(p[:, None] < p[None, :], 0.0, NEG)
    causal = np.where(p[None, :] <= p[:, None], 0.0, NEG)
    m = np.concatenate([strict, causal], axis=1).astype(np.float32)
    return c, m


def kernel(x, attn_norm_g, w_in, diff_qn_g, diff_kn_g, diff_lam, diff_subln_g, moba_qn_g, moba_kn_g,
           nsa_qn_g, nsa_kn_g, nsa_cmp_pe, nsa_cmp_w, w_gate, b_gate, w_branch, w_out, ffn_norm_g,
           w_ffn_gate, w_ffn_up, w_ffn_down):
    import concourse.bacc as bacc
    from concourse.bass_utils import run_bass_kernel_spmd as run

    L = DEPTH
    arr = lambda a: np.ascontiguousarray(a)
    columns = lambda g: np.asarray(g).reshape(L, KT, P).transpose(0, 2, 1)
    const, masks = constants()
    arrays = {
        "x": x, "w_in": w_in, "w_gate": w_gate, "w_branch": w_branch, "w_out": w_out,
        "w_ffn_gate": w_ffn_gate, "w_ffn_up": w_ffn_up, "w_ffn_down": w_ffn_down,
        "norm_g": np.concatenate([columns(attn_norm_g), columns(ffn_norm_g)], axis=2),
        "gains": np.concatenate([np.asarray(a).reshape(L, -1) for a in (
            diff_qn_g, diff_kn_g, moba_qn_g, moba_kn_g, nsa_qn_g, nsa_kn_g, diff_subln_g)], axis=1),
        "lam": np.asarray(diff_lam),
        "cmp_pe": np.asarray(nsa_cmp_pe).reshape(L, 2, 2, CMP_STRIDE, HD).transpose(0, 2, 4, 1, 3)
                    .reshape(L, P, 2, CMP_STRIDE),
        "cmp_w": np.asarray(nsa_cmp_w).reshape(L, 2, 2, CMP_STRIDE, HD, HD).transpose(0, 2, 4, 1, 3, 5)
                   .reshape(L, P, 2, CMP_STRIDE, HD),
        "b_gate": b_gate, "const": const, "masks": masks,
    }
    nc = bacc.Bacc("TRN2", target_bir_lowering=False, num_devices=1)
    feeds, args = {}, {}
    for name, a in arrays.items():
        a = arr(a)
        feeds[f"in_{name}"] = a
        args[name] = nc.dram_tensor(f"in_{name}", a.shape, mybir.dt.from_np(a.dtype), kind="ExternalInput").ap()
    out = nc.dram_tensor("out_x", (1, SEQ, D_MODEL), F32, kind="ExternalOutput").ap()
    trunk_kernel(nc, **args, out=out)
    r = run(nc, [feeds], core_ids=[0])
    return r.results[0]["out_x"]
```
